# Optimizing a Trainium2 kernel written in Bass

```python
import jax, jax.numpy as jnp
from jax import lax
import numpy as np

D_MODEL = 1024
BATCH = 1
SEQ = 1024
DEPTH = 1

ATTN_HEAD_DIM = 64
ATTN_HEADS_PER_GROUP = 4
ATTN_GROUPS = ((128, 1), (512, 4), (2048, 16))
N_ATTN_GROUPS = 3
ATTN_HEADS = ATTN_HEADS_PER_GROUP * N_ATTN_GROUPS
ATTN_WIDTH = ATTN_HEADS * ATTN_HEAD_DIM
ATTN_OUT_WIDTH = ATTN_HEADS_PER_GROUP * ATTN_HEAD_DIM
ATTN_BLOCK = 128

DN_HEADS = 4
DN_HEAD_DIM = 128
DN_WIDTH = DN_HEADS * DN_HEAD_DIM
DN_CONV = 4
DN_CHUNK = 64

D_FF = 2816
FFN_CONV = 3

NORM_EPS = 1e-6

IN_SIZES = (ATTN_WIDTH, ATTN_WIDTH, ATTN_WIDTH,
            3 * DN_WIDTH,
            DN_HEADS, DN_HEADS,
            DN_WIDTH,
            D_MODEL, D_MODEL)
IN_WIDTH = sum(IN_SIZES)

kernel_name = "hybrid_dilated_attn_gated_deltanet_convglu"

def rms_norm(x, w):
    x32 = x.astype(jnp.float32)
    y = x32 * lax.rsqrt(jnp.mean(x32 * x32, axis=-1, keepdims=True) + NORM_EPS)
    return (y * w.astype(jnp.float32)).astype(x.dtype)

def l2_norm(x):
    return x * lax.rsqrt(jnp.sum(x * x, axis=-1, keepdims=True) + NORM_EPS)

def causal_dwconv(x, w):
    K = w.shape[0]
    S = x.shape[1]
    xp = jnp.pad(x, ((0, 0), (K - 1, 0), (0, 0)))
    return sum(xp[:, j:j + S] * w[j] for j in range(K))

def dilated_window_attention(q, k, v, window, dilation):
    B, S, H, Dh = q.shape
    span = window // dilation
    L = S // dilation
    nb = -(-L // ATTN_BLOCK)
    Lp = nb * ATTN_BLOCK
    Bp = B * dilation

    def to_blocks(t):
        t = t.astype(jnp.float32).reshape(B, L, dilation, H, Dh).transpose(0, 2, 1, 3, 4)
        t = t.reshape(Bp, L, H, Dh)
        t = jnp.pad(t, ((0, 0), (0, Lp - L), (0, 0), (0, 0)))
        return t.reshape(Bp, nb, ATTN_BLOCK, H, Dh)

    qb, kb, vb = to_blocks(q), to_blocks(k), to_blocks(v)

    def band_keys(t):
        prev = jnp.pad(t[:, :-1], ((0, 0), (1, 0), (0, 0), (0, 0), (0, 0)))
        return jnp.concatenate([prev, t], axis=2)

    kw, vw = band_keys(kb), band_keys(vb)
    s = jnp.einsum('bnqhd,bnkhd->bnhqk', qb, kw) * (Dh ** -0.5)
    blk = jnp.arange(nb)[:, None] * ATTN_BLOCK
    qpos = blk + jnp.arange(ATTN_BLOCK)[None, :]
    kpos = blk - ATTN_BLOCK + jnp.arange(2 * ATTN_BLOCK)[None, :]
    rel = qpos[:, :, None] - kpos[:, None, :]
    valid = (rel >= 0) & (rel <= span) & (kpos[:, None, :] >= 0)
    s = jnp.where(valid[None, :, None], s, -jnp.inf)
    m = jnp.max(s, axis=-1, keepdims=True)
    p = jnp.exp(s - m)
    den = jnp.sum(p, axis=-1)
    o = jnp.einsum('bnhqk,bnkhd->bnqhd', p, vw) / jnp.swapaxes(den, 2, 3)[..., None]
    lse = jnp.swapaxes(m[..., 0] + jnp.log(den), 2, 3)

    o = o.reshape(Bp, Lp, H, Dh)[:, :L].reshape(B, dilation, L, H, Dh)
    o = o.transpose(0, 2, 1, 3, 4).reshape(B, S, H, Dh)
    lse = lse.reshape(Bp, Lp, H)[:, :L].reshape(B, dilation, L, H)
    lse = lse.transpose(0, 2, 1, 3).reshape(B, S, H)
    return o, lse

def gated_delta_rule_chunked(q, k, v, g, beta):
    B, S, H, dk = q.shape
    dv = v.shape[-1]
    C = DN_CHUNK
    N = S // C

    def chunk(t):
        return t.reshape(B, N, C, H, -1).transpose(0, 3, 1, 2, 4)

    qc, kc, vc = chunk(q), chunk(k), chunk(v)
    gc = jnp.cumsum(g.reshape(B, N, C, H).transpose(0, 3, 1, 2), axis=-1)
    bc = beta.reshape(B, N, C, H).transpose(0, 3, 1, 2)[..., None]
    kb, vb = kc * bc, vc * bc

    incl = jnp.tril(jnp.ones((C, C), dtype=bool))
    strict = jnp.tril(jnp.ones((C, C), dtype=bool), -1)
    decay = jnp.exp(jnp.where(incl, gc[..., :, None] - gc[..., None, :], -jnp.inf))

    M = jnp.where(strict, jnp.einsum('bhncd,bhnjd->bhncj', kb, kc) * decay, 0.0)
    A = jnp.eye(C, dtype=jnp.float32) + M
    rhs = jnp.concatenate([vb, kb * jnp.exp(gc)[..., None]], axis=-1)
    uw = lax.linalg.triangular_solve(A, rhs, left_side=True, lower=True, unit_diagonal=True)
    u, w = uw[..., :dv], uw[..., dv:]

    qk = jnp.einsum('bhncd,bhnjd->bhncj', qc, kc) * decay
    q_dec = qc * jnp.exp(gc)[..., None]
    k_dec = kc * jnp.exp(gc[..., -1:] - gc)[..., None]
    g_last = jnp.exp(gc[..., -1])

    def step(state, inp):
        u_i, w_i, qk_i, qd_i, kd_i, gl_i = inp
        v_new = u_i - jnp.einsum('bhcd,bhde->bhce', w_i, state)
        o_i = (jnp.einsum('bhcd,bhde->bhce', qd_i, state)
               + jnp.einsum('bhcj,bhje->bhce', qk_i, v_new))
        state = state * gl_i[..., None, None] + jnp.einsum('bhcd,bhce->bhde', kd_i, v_new)
        return state, o_i

    xs = tuple(jnp.moveaxis(t, 2, 0) for t in (u, w, qk, q_dec, k_dec, g_last))
    state0 = jnp.zeros((B, H, dk, dv), dtype=jnp.float32)
    _, o = lax.scan(step, state0, xs)
    return o.transpose(1, 0, 3, 2, 4).reshape(B, S, H, dv)

def hybrid_mixer(xn, w_in, dn_conv_w, dn_a_log, dn_dt_bias, dn_onorm_w, w_pa, w_pb, w_o):
    B, S, _ = xn.shape
    proj = xn @ w_in
    split_at = [int(i) for i in np.cumsum(IN_SIZES)[:-1]]
    aq, ak, av, dqkv, dbeta, da, dz, gate_a, gate_b = jnp.split(proj, split_at, axis=-1)

    hs = (B, S, N_ATTN_GROUPS, ATTN_HEADS_PER_GROUP, ATTN_HEAD_DIM)
    aq, ak, av = aq.reshape(hs), ak.reshape(hs), av.reshape(hs)
    outs, lses = [], []
    for gi, (window, dilation) in enumerate(ATTN_GROUPS):
        o_g, lse_g = dilated_window_attention(aq[:, :, gi], ak[:, :, gi], av[:, :, gi], window, dilation)
        outs.append(o_g)
        lses.append(lse_g)
    alpha = jax.nn.softmax(jnp.stack(lses, axis=0), axis=0)
    o_a = jnp.sum(alpha[..., None] * jnp.stack(outs, axis=0), axis=0)
    o_a = o_a.reshape(B, S, ATTN_OUT_WIDTH).astype(xn.dtype)

    dqkv = jax.nn.silu(causal_dwconv(dqkv, dn_conv_w)).astype(jnp.float32)
    dq, dk, dv = jnp.split(dqkv, 3, axis=-1)
    hd = (B, S, DN_HEADS, DN_HEAD_DIM)
    dq = l2_norm(dq.reshape(hd)) * (DN_HEAD_DIM ** -0.5)
    dk = l2_norm(dk.reshape(hd))
    dv = dv.reshape(hd)
    beta = jax.nn.sigmoid(dbeta.astype(jnp.float32))
    g = -jnp.exp(dn_a_log.astype(jnp.float32)) * jax.nn.softplus(
        da.astype(jnp.float32) + dn_dt_bias.astype(jnp.float32))
    o_b = gated_delta_rule_chunked(dq, dk, dv, g, beta)
    o_b = rms_norm(o_b, dn_onorm_w) * jax.nn.silu(dz.astype(jnp.float32).reshape(hd))
    o_b = o_b.reshape(B, S, DN_WIDTH).astype(xn.dtype)

    y = jax.nn.sigmoid(gate_a) * (o_a @ w_pa) + jax.nn.sigmoid(gate_b) * (o_b @ w_pb)
    return y @ w_o

def conv_glu_ffn(xn, w_up, conv_w, conv_b, w_down):
    h = causal_dwconv(xn @ w_up, conv_w) + conv_b
    gate, val = jnp.split(h, 2, axis=-1)
    return (jax.nn.silu(gate) * val) @ w_down

def setup_inputs(seed: int = 0) -> dict:
    key = jax.random.key(seed)
    ks = jax.random.split(key, 20)
    f32 = jnp.float32

    def nrm(k, shape, scale):
        return jax.random.normal(k, shape, f32) * scale

    dt = jnp.exp(jax.random.uniform(ks[5], (DEPTH, DN_HEADS), f32)
                 * (jnp.log(0.1) - jnp.log(0.001)) + jnp.log(0.001))
    return {
        "x": nrm(ks[0], (BATCH, SEQ, D_MODEL), 1.0),
        "norm1_w": 1.0 + nrm(ks[1], (DEPTH, D_MODEL), 0.02),
        "w_in": nrm(ks[2], (DEPTH, D_MODEL, IN_WIDTH), D_MODEL ** -0.5),
        "dn_conv_w": nrm(ks[3], (DEPTH, DN_CONV, 3 * DN_WIDTH), DN_CONV ** -0.5),
        "dn_a_log": jnp.log(jax.random.uniform(ks[4], (DEPTH, DN_HEADS), f32, 1.0, 16.0)),
        "dn_dt_bias": dt + jnp.log(-jnp.expm1(-dt)),
        "dn_onorm_w": 1.0 + nrm(ks[6], (DEPTH, DN_HEAD_DIM), 0.02),
        "w_pa": nrm(ks[7], (DEPTH, ATTN_OUT_WIDTH, D_MODEL), ATTN_OUT_WIDTH ** -0.5),
        "w_pb": nrm(ks[8], (DEPTH, DN_WIDTH, D_MODEL), DN_WIDTH ** -0.5),
        "w_o": nrm(ks[9], (DEPTH, D_MODEL, D_MODEL), D_MODEL ** -0.5),
        "norm2_w": 1.0 + nrm(ks[10], (DEPTH, D_MODEL), 0.02),
        "w_up": nrm(ks[11], (DEPTH, D_MODEL, 2 * D_FF), D_MODEL ** -0.5),
        "ffn_conv_w": nrm(ks[12], (DEPTH, FFN_CONV, 2 * D_FF), FFN_CONV ** -0.5),
        "ffn_conv_b": nrm(ks[13], (DEPTH, 2 * D_FF), 0.01),
        "w_down": nrm(ks[14], (DEPTH, D_FF, D_MODEL), D_FF ** -0.5),
        "final_norm_w": 1.0 + nrm(ks[15], (D_MODEL,), 0.02),
    }

def reference(x, norm1_w, w_in, dn_conv_w, dn_a_log, dn_dt_bias, dn_onorm_w, w_pa, w_pb, w_o,
              norm2_w, w_up, ffn_conv_w, ffn_conv_b, w_down, final_norm_w):
    for l in range(DEPTH):
        h = x + hybrid_mixer(rms_norm(x, norm1_w[l]), w_in[l], dn_conv_w[l], dn_a_log[l],
                             dn_dt_bias[l], dn_onorm_w[l], w_pa[l], w_pb[l], w_o[l])
        x = h + conv_glu_ffn(rms_norm(h, norm2_w[l]), w_up[l], ffn_conv_w[l], ffn_conv_b[l], w_down[l])
    return rms_norm(x, final_norm_w)


_drawn_inputs = setup_inputs


def setup_inputs(seed=0):
    import zlib

    import numpy as np

    out = dict(_drawn_inputs(seed))
    spreads = {}
    factors = {'norm1_w': 4.433,
     'dn_onorm_w': 7.956,
     'norm2_w': 13.966,
     'ffn_conv_b': 27.247,
     'final_norm_w': 8.183}
    for name, (base, spread) in spreads.items():
        noise = np.random.default_rng([zlib.crc32(name.encode()), seed]).standard_normal(out[name].shape)
        drawn = base * np.exp(spread * noise) if base else spread * noise
        out[name] = __import__('jax').numpy.asarray(drawn.astype(out[name].dtype))
    for name, factor in factors.items():
        out[name] = (out[name] * factor).astype(out[name].dtype)
    return out
```

```python
from contextlib import ExitStack

import concourse.bass as bass
from concourse import mybir

F32 = mybir.dt.float32
F32R = mybir.dt.float32r
ALU = mybir.AluOpType
ACT = mybir.ActivationFunctionType
AX = mybir.AxisListType.X

P = 128
S = 1024
D = 1024
NT = S // P
KT = D // P
HALF = 512
EPS = 1e-6

DH = 64
AH = 4
GROUPS = ((128, 1), (512, 4), (2048, 16))
NG = len(GROUPS)
AW = NG * AH * DH
AO = AH * DH
OC = DH + 2
ATT_SCALE = DH ** -0.5
NEG = -1.0e30

NH = 4
DK = 128
DW = NH * DK
CONV = 4
LEVELS = 7

FF = 2816
FT = FF // P
FCONV = 3

COL_Q, COL_K, COL_V = 0, AW, 2 * AW
COL_DN = 3 * AW
COL_BA = COL_DN + 3 * DW
COL_Z = COL_BA + 2 * NH
COL_GA = COL_Z + DW
COL_GB = COL_GA + D

PT_FFN = 0
PT_BIAS = FCONV * 2 * FT
PT_DN = PT_BIAS + 2 * FT
PT_N1 = PT_DN + CONV * 3 * NH
PT_N2 = PT_N1 + KT
PT_COLS = PT_N2 + KT


def mixer_jobs():
    jobs = [("ba", 0, COL_BA)]
    jobs += [("conv", t, COL_DN + t * P) for t in range(3 * NH)]
    jobs += [("z", t, COL_Z + t * P) for t in range(NH)]
    for g in range(NG):
        for kind, col in (("q", COL_Q), ("k", COL_K), ("v", COL_V)):
            jobs += [(kind, 2 * g + t, col + (2 * g + t) * P) for t in range(2)]
    jobs += [("ga", t, COL_GA + t * P) for t in range(KT)]
    return jobs


def dn_stages():
    out = []
    for c in range(NT):
        seq = ["kv", "kT", "kkD", "kq", "P0", "U0"]
        for lv in range(1, LEVELS):
            seq += [f"P{lv}", f"T{lv}"]
        seq += ["uw", "sq", "so"]
        seq = [(name, c) for name in seq]
        if c:
            seq.insert(4, ("ob", c - 1))
        out += seq
    return out + [("ob", NT - 1)]


def att_units():
    return [(g, i) for g in range(NG) for i in range(NT)]


def mixer_schedule(jobs):
    dn = dn_stages()
    items = [("w", 0)]
    ready = []
    units = att_units()
    combine = [("cmb", i) for i in range(NT)]
    for n, (kind, t, _) in enumerate(jobs):
        for k in range(KT):
            items.append(("mm", n, k))
            if k == 0 and n + 1 < len(jobs):
                items.append(("w", n + 1))
            if n and k == 2:
                pk, pt, _ = jobs[n - 1]
                if pk == "ba":
                    items += [("gates",), ("gatesum",)]
                if pk == "conv":
                    items.append(("silu", n - 1))
                if pk == "v":
                    items.append(("vT", pt))
                    if pt % 2:
                        g = pt // 2
                        for u in units:
                            if u[0] == g:
                                ready += [("a_qk", u), ("a_pT", u), ("a_pv", u)]
            if n and k == 6 and jobs[n - 1][0] == "conv" and jobs[n - 1][1] < 2 * NH:
                items.append(("ssq", jobs[n - 1][1]))
            if kind == "conv" and t == 2 * NH + 1 and k == 4:
                items.append(("rnorm",))
            if n > 1 + 3 * NH and dn:
                items.append(("dn",) + dn.pop(0))
            if ready and (k % 2 == 0 or kind == "ga"):
                items.append(ready.pop(0))
            elif kind == "ga" and not ready and k % 3 == 0 and combine:
                items.append(combine.pop(0))
        items.append(("evac", n))
    assert not dn and not ready
    return items + combine


def count(seq):
    return {key: n + 1 for n, key in enumerate(seq)}


def build(nc, x, norm1_w, w_in, dn_conv_w, dn_a_log, dn_dt_bias, dn_onorm_w, w_pa, w_pb, w_o,
          norm2_w, w_up, ffn_conv_w, ffn_conv_b, w_down, final_norm_w, out):
    xd = x[0]
    outd = out[0]
    w_in2, w_pa2, w_pb2, w_o2, w_up2, w_dn2 = w_in[0], w_pa[0], w_pb[0], w_o[0], w_up[0], w_down[0]
    conv_d = nc.dram_tensor("conv_d", [4 * NH, P, S], F32, kind="Internal").ap()
    og_d = nc.dram_tensor("og_d", [NG, S, AH * OC], F32, kind="Internal").ap()
    oa_d = nc.dram_tensor("oa_d", [2, P, S], F32, kind="Internal").ap()
    ob_d = nc.dram_tensor("ob_d", [NH, P, S], F32, kind="Internal").ap()
    sga_d = nc.dram_tensor("sga_d", [KT, P, S], F32, kind="Internal").ap()
    h_d = nc.dram_tensor("h_d", [S, D], F32, kind="Internal").ap()

    with ExitStack() as top:
        top.enter_context(nc.allow_non_contiguous_dma(reason="a few small parameter rows"))

        def sem(name):
            return top.enter_context(nc.semaphore(name))

        def psum(name, cols=HALF):
            return top.enter_context(nc.psum_tensor(name, [P, cols], F32))

        def sb(ctx, name, shape, dt=F32):
            return ctx.enter_context(nc.sbuf_tensor(name, shape, dt))

        acc = [psum("acc0", S), psum("acc1", S)]
        bank_a, bank_b = psum("bank_a"), psum("bank_b")
        att_ps = psum("att_ps", S)
        every = [acc[0][:, 0:HALF], acc[0][:, HALF:S], acc[1][:, 0:HALF], acc[1][:, HALF:S],
                 bank_a[:, :], bank_b[:, :], att_ps[:, 0:HALF], att_ps[:, HALF:S]]

        ident = sb(top, "ident", [P, P])
        ones = sb(top, "ones", [P, P])
        prm = sb(top, "prm", [P, PT_COLS])
        small = sb(top, "small", [P, 32])
        xh = sb(top, "xh", [P, KT, S], F32R)
        xl = sb(top, "xl", [P, KT, S], F32R)
        norm_in(nc, sem, sb, every, xd, norm1_w, norm2_w, dn_conv_w, ffn_conv_w, ffn_conv_b,
                ident, ones, prm, small, xh, xl)
        mixer(nc, sem, sb, acc, bank_a, bank_b, att_ps, ident, ones, prm, xh, xl,
              w_in2, dn_a_log, dn_dt_bias, dn_onorm_w, conv_d, og_d, oa_d, ob_d, sga_d)
        with ExitStack() as late:
            y = sb(late, "y", [P, KT, S])
            merge(nc, sem, sb, acc, att_ps, xh, xl, y, w_in2, w_pa2, w_pb2, oa_d, ob_d, sga_d)
            project_out(nc, sem, sb, every, ident, prm, small, xh, xl, y, w_o2, xd, h_d)
        ffn(nc, sem, sb, acc, every, prm, small, xh, xl, w_up2, w_dn2, h_d, final_norm_w, outd)


def norm_in(nc, sem, sb, every, xd, norm1_w, norm2_w, dn_conv_w, ffn_conv_w, ffn_conv_b,
            ident, ones, prm, small, xh, xl):
    ss, ms, rstd, mhalf = small[:, 0:8], small[:, 8:16], small[:, 16:24], small[:, 24:32]
    s_x, s_par = sem("n_x_loaded"), sem("n_params_loaded")
    s_par0 = sem("n_stage_zeroed")
    s_id, s_const = sem("n_const_step"), sem("n_constants_ready")
    s_sq, s_ms, s_rstd, s_xn = sem("n_squares"), sem("n_mean_square"), sem("n_rstd"), sem("n_scaled")
    s_ps, s_hi, s_lo, s_prm, s_prt = (sem("n_transposed"), sem("n_high"), sem("n_low"), sem("n_params_ready"),
                                      sem("n_params_transposed"))
    with ExitStack() as ctx:
        xs = sb(ctx, "xs", [P, NT, D])
        junk = sb(ctx, "junk", [P, D])
        rows = 2 * FT
        stage = sb(ctx, "stage", [rows, 10, P])
        table = [(PT_FFN + j * rows, rows, j) for j in range(FCONV)] + [(PT_BIAS, rows, FCONV)]
        table += [(PT_DN + j * 3 * NH, 3 * NH, 4 + j) for j in range(CONV)]
        table += [(PT_N1, KT, 8), (PT_N2, KT, 9)]
        with nc.Block() as block:

            @block.sync
            def _(sp):
                for i in range(NT):
                    sp.dma_start(xs[:, i, :], xd[i * P:(i + 1) * P, :]).then_inc(s_x, 16)

            @block.scalar
            def _(act):
                for j in range(FCONV):
                    act.dma_start(stage[:, j, :], ffn_conv_w[0, j].rearrange("(m p) -> m p", p=P)).then_inc(s_par, 16)
                act.dma_start(stage[:, FCONV, :], ffn_conv_b[0].rearrange("(m p) -> m p", p=P)).then_inc(s_par, 16)
                for j in range(CONV):
                    act.dma_start(stage[0:3 * NH, 4 + j, :],
                                  dn_conv_w[0, j].rearrange("(m p) -> m p", p=P)).then_inc(s_par, 16)
                act.dma_start(stage[0:KT, 8, :], norm1_w[0].rearrange("(m p) -> m p", p=P)).then_inc(s_par, 16)
                act.dma_start(stage[0:KT, 9, :], norm2_w[0].rearrange("(m p) -> m p", p=P)).then_inc(s_par, 16)
                for i in range(NT):
                    act.wait_ge(s_x, 16 * NT)
                    if i:
                        act.wait_ge(s_sq, i)
                    nc.scalar.activation(junk[:], xs[:, i, :], ACT.Square, accum_out=ss[:, i:i + 1]).then_inc(s_sq, 1)
                act.wait_ge(s_prm, 1)
                for u in range(2 * KT):
                    k, half = u // 2, u % 2
                    act.wait_ge(s_ps, u + 1)
                    nc.scalar.activation(xh[:, k, half * HALF:(half + 1) * HALF], every[u % 8], ACT.Copy,
                                         scale=prm[:, PT_N1 + k:PT_N1 + k + 1]).then_inc(s_hi, 1)

            @block.gpsimd
            def _(pool):
                nc.gpsimd.memset(mhalf, -0.5).then_inc(s_id, 1)
                nc.gpsimd.memset(ones[:], 1.0).then_inc(s_id, 1)
                nc.gpsimd.memset(ident[:], 0.0).then_inc(s_id, 1)
                pool.wait_ge(s_id, 3)
                nc.gpsimd.affine_select(out=ident[:], in_=ident[:], compare_op=ALU.not_equal, fill=1.0, base=0,
                                        pattern=[[-1, P]], channel_multiplier=1).then_inc(s_const, 1)
                for i in range(NT):
                    pool.wait_ge(s_ms, i + 1)
                    nc.gpsimd.tensor_tensor(rstd[:, i:i + 1], ms[:, i:i + 1], mhalf[:, 0:1], ALU.pow).then_inc(s_rstd, 1)

            @block.vector
            def _(dve):
                for i in range(NT):
                    dve.wait_ge(s_sq, i + 1)
                    nc.vector.tensor_scalar(ms[:, i:i + 1], ss[:, i:i + 1], 1.0 / D, EPS, ALU.mult,
                                            ALU.add).then_inc(s_ms, 1)
                    if i:
                        dve.wait_ge(s_rstd, i)
                        nc.vector.tensor_scalar(xs[:, i - 1, :], xs[:, i - 1, :], rstd[:, i - 1:i], None,
                                                ALU.mult).then_inc(s_xn, 1)
                dve.wait_ge(s_rstd, NT)
                nc.vector.tensor_scalar(xs[:, NT - 1, :], xs[:, NT - 1, :], rstd[:, NT - 1:NT], None,
                                        ALU.mult).then_inc(s_xn, 1)
                dve.wait_ge(s_prt, 1)
                nc.vector.tensor_copy(prm[:], every[7][:, 0:PT_COLS]).then_inc(s_prm, 1)
                dve.wait_ge(s_prm, 1)
                for u in range(2 * KT):
                    k, half = u // 2, u % 2
                    dve.wait_ge(s_hi, u + 1)
                    cols = slice(half * HALF, (half + 1) * HALF)
                    nc.vector.scalar_tensor_tensor(xl[:, k, cols], every[u % 8], prm[:, PT_N1 + k:PT_N1 + k + 1],
                                                   xh[:, k, cols].bitcast(F32), ALU.mult,
                                                   ALU.subtract).then_inc(s_lo, 1)

            @block.tensor
            def _(pe):
                pe.wait_ge(s_const, 1)
                pe.wait_ge(s_par, 16 * 10)
                for n, (col, m, j) in enumerate(table):
                    last = nc.tensor.transpose(every[7][:, col:col + m], stage[0:m, j, :], ident[0:m, 0:m])
                last.then_inc(s_prt, 1)
                for u in range(2 * KT):
                    k, half = u // 2, u % 2
                    pe.wait_ge(s_xn, 4 * (half + 1) if u < 2 else NT)
                    if u == 7:
                        pe.wait_ge(s_prm, 1)
                    if u >= 8:
                        pe.wait_ge(s_lo, u - 7)
                    for q in range(4):
                        last = nc.tensor.transpose(every[u % 8][:, q * P:(q + 1) * P],
                                                   xs[:, half * 4 + q, k * P:(k + 1) * P], ident[:])
                    last.then_inc(s_ps, 1)


def product3(nc, out, wh, wl, xh, xl, halves, first, last):
    n = 0
    parts = [(wh, xh), (wh, xl), (wl, xh)]
    for j, (w, xx) in enumerate(parts):
        for lo, hi in halves:
            mm = nc.tensor.matmul(out[:, lo:hi], w, xx[:, lo:hi], start=first and j == 0, stop=last and j == 2)
    return mm


HALVES = ((0, HALF), (HALF, S))


def mixer(nc, sem, sb, acc, bank_a, bank_b, att_ps, ident, ones, prm, xh, xl,
          w_in2, dn_a_log, dn_dt_bias, dn_onorm_w, conv_d, og_d, oa_d, ob_d, sga_d):
    jobs = mixer_jobs()
    items = mixer_schedule(jobs)
    NJ = len(jobs)
    conv_no = count([n for n, j in enumerate(jobs) if j[0] in ("conv", "z")])
    job_no = {(kind, t): n for n, (kind, t, _) in enumerate(jobs)}

    use_a = {"kv", "kT", "kkD", "kq", "uw", "sq", "so", "ob"} | {f"P{lv}" for lv in range(LEVELS)}
    use_a |= {f"T{lv}" for lv in range(1, LEVELS - 1)}
    use_b = {"kv", "kkD", "U0", "uw", "sq", "so"} | {f"T{lv}" for lv in range(1, LEVELS)}
    dn = [it[1:] for it in items if it[0] == "dn"]
    dn_done = count(dn)
    a_taken = count([d for d in dn if d[0] in use_a])
    b_taken = count([d for d in dn if d[0] in use_b])
    att_no = count([it for it in items if it[0] in ("gates", "gatesum", "vT", "a_qk", "a_pT", "a_pv", "cmb")])
    order = {it: n for n, it in enumerate(items)}
    unit_no = count(att_units())
    stores = [u for u in att_units() for _ in range(2 if u[0] == 2 else 1)]
    o_stored = {u: 16 * (n + 1) for n, u in enumerate(stores)}
    for g in range(NG - 1):
        nxt = order[("evac", job_no[("q", 2 * g + 4)] if g + 2 < NG else job_no[("ga", 0)])]
        assert order[("a_qk", (g, NT - 1))] < nxt
        assert g + 2 >= NG or order[("a_pv", (g, NT - 1))] < order[("vT", 2 * g + 4)]

    s_const, s_masks, s_small = sem("m_const_step"), sem("m_masks_ready"), sem("m_small_loaded")
    s_raw = [sem("m_w_loaded0"), sem("m_w_loaded1")]
    s_whi, s_wlo = sem("m_w_high"), sem("m_w_low")
    s_acc, s_taken = sem("m_acc_done"), sem("m_acc_taken")
    s_tap0, s_tap, s_silu = sem("m_tap0"), sem("m_tap"), sem("m_silu_done")
    s_cst = [sem("m_conv_stored0"), sem("m_conv_stored1")]
    s_sqr, s_ssq, s_ssum, s_rr = sem("m_squares"), sem("m_ssq_summed"), sem("m_ssq_read"), sem("m_norms")
    s_atpe, s_attk = sem("m_att_filled"), sem("m_att_taken")
    s_bact, s_link, s_gready = sem("m_gate_act"), sem("m_dve_link"), sem("m_gates_ready")
    s_dn, s_a, s_b = sem("m_dn_filled"), sem("m_bank_a_taken"), sem("m_bank_b_taken")
    s_ckkv, s_ckq, s_ckz = sem("m_chunk_kv"), sem("m_chunk_q"), sem("m_chunk_z")
    s_gu, s_kk, s_dtm, s_lm = sem("m_gu"), sem("m_kbe_kd"), sem("m_decay_masked"), sem("m_level_masked")
    s_t0, s_sd, s_osq = sem("m_t0"), sem("m_state_decayed"), sem("m_o_squares")
    s_ov, s_on = sem("m_o_variance"), sem("m_o_normed")
    s_obst = sem("m_ob_stored")
    s_nm, s_p, s_o, s_ost = sem("m_neg_max"), sem("m_probs"), sem("m_o_ready"), sem("m_o_stored")
    s_cl = [sem("m_cmb_loaded0"), sem("m_cmb_loaded1")]
    s_cd, s_ce, s_co, s_cs = sem("m_cmb_diff"), sem("m_cmb_exp"), sem("m_cmb_out"), sem("m_cmb_stored")
    s_sgs = [sem("m_sga_stored0"), sem("m_sga_stored1")]

    with ExitStack() as ctx:
        U = sb(ctx, "U", [P, P])
        Ls = sb(ctx, "Ls", [P, P])
        lmask = sb(ctx, "lmask", [P, LEVELS, P])
        amask = sb(ctx, "amask", [P, 2 * P])
        dmask = sb(ctx, "dmask", [P, P])
        onw = sb(ctx, "onw", [P, 1])
        alog = sb(ctx, "alog", [P, NH])
        dtb = sb(ctx, "dtb", [P, NH])
        raw = sb(ctx, "raw", [P, 2, KT, P])
        wh = sb(ctx, "wh", [P, 2, KT, P], F32R)
        wl = sb(ctx, "wl", [P, 2, KT, P], F32R)
        g_all = sb(ctx, "g_all", [P, NT, NH])
        beta = sb(ctx, "beta", [P, NT, NH])
        dec = sb(ctx, "dec", [P, 3, NT, NH])
        bE = sb(ctx, "bE", [P, NT, NH])
        rr = sb(ctx, "rr", [P, 2, NH, NT])
        rqs = sb(ctx, "rqs", [P, NH, NT])
        rq2 = sb(ctx, "rq2", [P, NH, NT])
        tiny = sb(ctx, "tiny", [P, 4, NH])
        hp64 = sb(ctx, "hp64", [P, 2 * NH * NT])
        eg, ekd, egl = dec[:, 0], dec[:, 1], dec[:, 2]
        ck = sb(ctx, "ck", [P, 4 * NH, P])
        kh, vb, kbe, kd, X1, Pb, DTm, WT, KQd, Lm0, Lm1, Ub, St, o1, sqo, on, obt = (
            sb(ctx, "d_" + name, [P, NH, P]) for name in
            ("kh", "vb", "kbe", "kd", "khT_T_u", "gU_P_vn", "DTm_Sd", "WT_wT", "KQd", "Lm0", "Lm1", "U", "S",
             "o", "sqo", "on", "obt"))
        Lm = (Lm0, Lm1)
        V = [sb(ctx, f"V{j}", [P, NT, AH, DH + 1]) for j in range(2)]
        vt = sb(ctx, "vt", [P, S])
        sc = sb(ctx, "sc", [P, AH, 2 * P])
        mx = sb(ctx, "mx", [P, 2, AH])
        O = sb(ctx, "O", [P, AH, OC])
        PT = sb(ctx, "PT", [P, AH * 2, P])
        cbs = sb(ctx, "cbs", [P, 4, NG, AH])
        cbm = sb(ctx, "cbm", [P, 3, AH])
        with ExitStack() as early:
            cs = sb(early, "cs", [P, 2, S])
            so = sb(early, "so", [P, 2, S])
            sqb = sb(early, "sqb", [P, S])
            bas = sb(early, "bas", [P, S])
            bat = sb(early, "bat", [P, 6, NT, 2 * NH])
        qk = [sb(ctx, f"qk{j}", [P, 4, S]) for j in range(2)]
        cb = [qk[1][:, j, 0:NG * AH * OC].rearrange("p (g h c) -> p g h c", g=NG, h=AH) for j in range(2)]
        sga = [qk[1][:, 2 + j, :] for j in range(2)]
        ocb = PT[:, 0:2, :].rearrange("p a c -> p (a c)")
        oat = PT[:, 4:6, :]

        def bc(ap):
            return ap.unsqueeze(2).to_broadcast([P, NH, P])

        def bh(ap):
            return ap.unsqueeze(1).to_broadcast([P, NH, P])

        A4 = bank_a[:, :].rearrange("p (h c) -> p h c", h=NH)
        B4 = bank_b[:, :].rearrange("p (h c) -> p h c", h=NH)
        att0 = att_ps[:, 0:HALF]
        att4 = att_ps[:, :].rearrange("p (h c) -> p h c", h=AH)

        def dilated(ap, g):
            return ap.rearrange("p (l r) -> p r l", r=GROUPS[g][1])

        def residues(ap, g):
            return ap.rearrange("p (r l) -> p r l", r=GROUPS[g][1])

        def key_tiles(g, i):
            if (g == 0 and i) or (g == 1 and i % 2):
                return [i - 1, i]
            return [i]

        def slot(h):
            return 2 * (h % 2) + h // 2

        with nc.Block() as block:

            @block.sync
            def _(sp):
                sp.dma_start(onw[:], dn_onorm_w[0].rearrange("(p o) -> p o", o=1)).then_inc(s_small, 16)
                sp.dma_start(alog[:], dn_a_log.to_broadcast([P, NH])).then_inc(s_small, 16)
                sp.dma_start(dtb[:], dn_dt_bias.to_broadcast([P, NH])).then_inc(s_small, 16)

                def load_w(n):
                    if n >= 2:
                        sp.wait_ge(s_wlo, n - 1)
                    col = jobs[n][2]
                    sp.dma_start(raw[:, n % 2],
                                 w_in2[:, col:col + P].rearrange("(k p) c -> p k c", p=P)).then_inc(s_raw[n % 2], 16)

                def load_chunk(first, tiles, c, loaded):
                    sp.dma_start(ck[:, first:first + tiles, :],
                                 conv_d[first:first + tiles, :, c * P:(c + 1) * P].rearrange("t p c -> p t c")
                                 ).then_inc(loaded, 16)

                load_w(0)
                for it in items:
                    kind = it[0]
                    if kind == "w" and it[1] + 1 < NJ:
                        load_w(it[1] + 1)
                    if kind == "silu":
                        n, t = it[1], jobs[it[1]][1]
                        sp.wait_ge(s_silu, conv_no[n])
                        sp.dma_start(conv_d[t], so[:, conv_no[n] % 2, :]).then_inc(s_cst[conv_no[n] % 2], 16)
                    if kind == "evac" and jobs[it[1]][0] == "z":
                        n, t = it[1], jobs[it[1]][1]
                        sp.wait_ge(s_taken, n + 1)
                        sp.dma_start(conv_d[3 * NH + t], so[:, conv_no[n] % 2, :]).then_inc(s_cst[conv_no[n] % 2], 16)
                        if t == NH - 1:
                            for j in range(2):
                                sp.wait_ge(s_cst[j], 16 * 2 * NH)
                            load_chunk(3 * NH, NH, 0, s_ckz)
                    if kind == "dn":
                        name, c = it[1:]
                        if name == "kv" and c == 0:
                            for j in range(2):
                                sp.wait_ge(s_cst[j], 16 * 3 * NH // 2)
                            load_chunk(NH, 2 * NH, 0, s_ckkv)
                            load_chunk(0, NH, 0, s_ckq)
                        if name == "kT" and c + 1 < NT:
                            sp.wait_ge(s_dn, dn_done[("kv", c)])
                            load_chunk(NH, 2 * NH, c + 1, s_ckkv)
                        if name == "so" and c + 1 < NT:
                            sp.wait_ge(s_dn, dn_done[("sq", c)])
                            load_chunk(0, NH, c + 1, s_ckq)
                        if name == "ob":
                            sp.wait_ge(s_a, a_taken[(name, c)])
                            sp.dma_start(ob_d[:, :, c * P:(c + 1) * P].rearrange("h p c -> p h c"),
                                         obt[:]).then_inc(s_obst, 16)
                            if c + 1 < NT:
                                load_chunk(3 * NH, NH, c + 1, s_ckz)
                    if kind == "a_pv":
                        g, i = it[1]
                        sp.wait_ge(s_o, unit_no[(g, i)])
                        rows = og_d[g].rearrange("(l r) c -> r l c", r=GROUPS[g][1])
                        src = O[:].rearrange("p h c -> p (h c)")
                        if g == 0:
                            sp.dma_start(rows[0, i * P:(i + 1) * P, :], src).then_inc(s_ost, 16)
                        elif g == 1:
                            sp.dma_start(rows[i // 2, (i % 2) * P:(i % 2 + 1) * P, :], src).then_inc(s_ost, 16)
                        else:
                            for j in range(2):
                                sp.dma_start(rows[2 * i + j], src[j * 64:(j + 1) * 64, :]).then_inc(s_ost, 16)
                    if kind == "evac" and jobs[it[1]][0] == "ga":
                        m = jobs[it[1]][1]
                        sp.wait_ge(s_taken, it[1] + 1)
                        sp.dma_start(sga_d[m], sga[m % 2]).then_inc(s_sgs[m % 2], 16)
                    if kind == "cmb":
                        i = it[1]
                        if i == 0:
                            sp.wait_ge(s_ost, o_stored[(NG - 1, NT - 1)])
                        for j in ([0, 1] if i == 0 else [i + 1] if i + 1 < NT else []):
                            if j >= 2:
                                sp.wait_ge(s_co, j - 1)
                            sp.dma_start(cb[j % 2].rearrange("p g h c -> p g (h c)"),
                                         og_d[:, j * P:(j + 1) * P, :].rearrange("g t c -> t g c")
                                         ).then_inc(s_cl[j % 2], 16)
                        sp.wait_ge(s_attk, att_no[it])
                        sp.dma_start(oa_d[:, :, i * P:(i + 1) * P].rearrange("a p c -> p a c"), oat).then_inc(s_cs, 16)
                sp.wait_ge(s_cs, 16 * NT)
                for j in range(2):
                    sp.wait_ge(s_sgs[j], 16 * KT // 2)
                sp.wait_ge(s_obst, 16 * NT)

            @block.gpsimd
            def _(pool):
                g = nc.gpsimd
                steps = 0

                def step(ins):
                    nonlocal steps
                    steps += 1
                    ins.then_inc(s_const, 1)
                    pool.wait_ge(s_const, steps)

                step(g.memset(U[:], 1.0))
                step(g.memset(Ls[:], 1.0))
                step(g.memset(hp64[:], -0.5))
                step(g.affine_select(out=U[:], in_=U[:], compare_op=ALU.is_ge, fill=0.0, base=0, pattern=[[1, P]],
                                     channel_multiplier=-1))
                step(g.affine_select(out=Ls[:], in_=Ls[:], compare_op=ALU.is_gt, fill=0.0, base=0, pattern=[[-1, P]],
                                     channel_multiplier=1))
                step(g.memset(lmask[:], 0.0))
                for lv in range(LEVELS):
                    size = 1 << lv
                    nb = P // (2 * size)
                    v = lmask[:, lv, :].rearrange("p (b t s) -> p b t s", t=2, s=size)[:, :, 1, :]
                    step(g.memset(v, 1.0))
                    step(g.affine_select(out=v, in_=v, compare_op=ALU.is_ge, fill=0.0, base=0,
                                         pattern=[[-2 * size, nb], [0, size]], channel_multiplier=1))
                    step(g.affine_select(out=v, in_=v, compare_op=ALU.is_gt, fill=0.0, base=size,
                                         pattern=[[2 * size, nb], [0, size]], channel_multiplier=-1))
                step(g.memset(amask[:], 0.0))
                step(g.affine_select(out=amask[:], in_=amask[:], compare_op=ALU.is_ge, fill=NEG, base=0,
                                     pattern=[[1, 2 * P]], channel_multiplier=-1))
                step(g.affine_select(out=amask[:], in_=amask[:], compare_op=ALU.is_ge, fill=NEG, base=P,
                                     pattern=[[-1, 2 * P]], channel_multiplier=1))
                step(g.memset(dmask[:], 0.0))
                step(g.affine_select(out=dmask[:], in_=dmask[:], compare_op=ALU.is_ge, fill=NEG, base=0,
                                     pattern=[[-1, P]], channel_multiplier=1))
                step(g.affine_select(out=dmask[:, 0:64], in_=dmask[:, 0:64], compare_op=ALU.is_ge, fill=NEG, base=63,
                                     pattern=[[0, 64]], channel_multiplier=-1))
                step(g.memset(St[:], 0.0))
                for j in range(2):
                    step(g.memset(V[j][:, :, :, DH:DH + 1], 1.0))
                g.memset(tiny[:], 0.0).then_inc(s_masks, 1)

                def level_mask(lv, c):
                    g.tensor_tensor(Lm[lv % 2][:], WT[:], bh(lmask[:, lv, :]), ALU.mult).then_inc(s_lm, 1)

                def out_norm(c):
                    pool.wait_ge(s_ov, 2 * c + 2)
                    g.tensor_tensor(tiny[:, 2, :], tiny[:, 1, :], hp64[:, 0:NH], ALU.pow).then_inc(s_on, 1)
                    pool.wait_ge(s_on, 3 * c + 1)
                    g.tensor_tensor(tiny[:, 3, :], tiny[:, 2, :], rqs[:, :, c], ALU.mult).then_inc(s_on, 1)
                    pool.wait_ge(s_on, 3 * c + 2)
                    if c:
                        pool.wait_ge(s_dn, dn_done[("ob", c - 1)])
                    g.tensor_tensor(on[:], o1[:], bc(tiny[:, 3, :]), ALU.mult).then_inc(s_on, 1)

                for it in items:
                    kind = it[0]
                    if kind == "w":
                        n = it[1]
                        pool.wait_ge(s_whi, n + 1)
                        g.tensor_tensor(wl[:, n % 2], raw[:, n % 2], wh[:, n % 2].bitcast(F32),
                                        ALU.subtract).then_inc(s_wlo, 1)
                    if kind == "silu" and jobs[it[1]][1] < 2 * NH:
                        n, t = it[1], jobs[it[1]][1]
                        pool.wait_ge(s_silu, conv_no[n])
                        if t:
                            pool.wait_ge(s_ssq, t)
                        g.tensor_tensor(sqb[:], so[:, conv_no[n] % 2, :], so[:, conv_no[n] % 2, :],
                                        ALU.mult).then_inc(s_sqr, 1)
                    if kind == "rnorm":
                        pool.wait_ge(s_ssum, 1)
                        flat = rr[:].rearrange("p a h c -> p (a h c)")
                        g.tensor_tensor(flat, flat, hp64[:], ALU.pow).then_inc(s_rr, 1)
                        pool.wait_ge(s_rr, 1)
                        g.tensor_scalar(rqs[:], rr[:, 0], DK ** -0.5, 0.0, ALU.mult, ALU.add).then_inc(s_rr, 1)
                        pool.wait_ge(s_rr, 2)
                        g.tensor_tensor(rq2[:], rqs[:], rqs[:], ALU.mult).then_inc(s_rr, 1)
                        pool.wait_ge(s_rr, 3)
                        g.tensor_scalar(rq2[:], rq2[:], 1.0 / DK, 0.0, ALU.mult, ALU.add).then_inc(s_rr, 1)
                    if kind == "dn":
                        name, c = it[1:]
                        if name == "kv":
                            if c == 0:
                                pool.wait_ge(s_gready, 1)
                            else:
                                pool.wait_ge(s_dn, dn_done[("so", c - 1)])
                            g.tensor_tensor(Pb[:], bh(U[:]), bc(g_all[:, c, :]), ALU.mult).then_inc(s_gu, 1)
                            pool.wait_ge(s_a, a_taken[("kv", c)])
                            g.tensor_tensor(kbe[:], kh[:], bc(bE[:, c, :]), ALU.mult)
                            g.tensor_tensor(kd[:], kh[:], bc(ekd[:, c, :]), ALU.mult).then_inc(s_kk, 1)
                        if name == "kkD":
                            pool.wait_ge(s_b, b_taken[(name, c)])
                            g.tensor_tensor(DTm[:], DTm[:], bh(U[:]), ALU.mult).then_inc(s_dtm, 1)
                            pool.wait_ge(s_a, a_taken[(name, c)])
                            level_mask(0, c)
                            level_mask(1, c)
                        if name[0] == "P" and int(name[1:]) + 2 < LEVELS:
                            pool.wait_ge(s_dn, dn_done[(name, c)])
                            level_mask(int(name[1:]) + 2, c)
                        if name == "uw":
                            pool.wait_ge(s_a, a_taken[("kq", c)])
                            g.tensor_tensor(DTm[:], St[:], bc(egl[:, c, :]), ALU.mult).then_inc(s_sd, 1)
                        if name == "so":
                            pool.wait_ge(s_b, b_taken[(name, c)])
                            g.tensor_tensor(sqo[:], o1[:], o1[:], ALU.mult).then_inc(s_osq, 1)
                        if name == "kT" and c:
                            out_norm(c - 1)
                        if name == "ob" and c == NT - 1:
                            out_norm(c)

            @block.scalar
            def _(act):
                g = nc.scalar
                for it in items:
                    kind = it[0]
                    if kind == "w":
                        n = it[1]
                        act.wait_ge(s_raw[n % 2], 16 * (n // 2 + 1))
                        if n >= 2:
                            act.wait_ge(s_acc, n - 1)
                        g.activation(wh[:, n % 2], raw[:, n % 2], ACT.Copy).then_inc(s_whi, 1)
                    if kind == "evac":
                        n = it[1]
                        jk, t, _ = jobs[n]
                        a = acc[n % 2]
                        act.wait_ge(s_acc, n + 1)
                        if n:
                            act.wait_ge(s_taken, n)
                        if jk == "ba":
                            g.activation(bas[0:2 * NH, :], a[0:2 * NH, :], ACT.Copy).then_inc(s_taken, 1)
                        if jk == "conv":
                            w = PT_DN + (CONV - 1) * 3 * NH + t
                            g.activation(cs[:, conv_no[n] % 2, :], a[:], ACT.Copy,
                                         scale=prm[:, w:w + 1]).then_inc(s_tap0, 1)
                        if jk == "z":
                            m = conv_no[n]
                            act.wait_ge(s_cst[m % 2], 16 * ((m - 1) // 2))
                            g.activation(so[:, m % 2, :], a[:], ACT.Silu).then_inc(s_taken, 1)
                        if jk in ("q", "k"):
                            grp = t // 2
                            if jk == "q" and t == 0:
                                for j in range(2):
                                    act.wait_ge(s_cst[j], 16 * 2 * NH)
                                act.wait_ge(s_ssq, 2 * NH)
                                act.wait_ge(s_gready, 1)
                            if jk == "q" and grp == 2:
                                act.wait_ge(s_atpe, att_no[("a_qk", (0, NT - 1))])
                            g.activation(residues(qk[grp % 2][:, (0 if jk == "q" else 2) + t % 2, :], grp),
                                         dilated(a[:], grp), ACT.Copy).then_inc(s_taken, 1)
                        if jk == "v":
                            if t:
                                act.wait_ge(s_atpe, att_no[("vT", t - 1)])
                            g.activation(residues(vt[:], t // 2), dilated(a[:], t // 2), ACT.Copy).then_inc(s_taken, 1)
                        if jk == "ga":
                            if t == 0:
                                act.wait_ge(s_atpe, att_no[("a_qk", (1, NT - 1))])
                            if t >= 2:
                                act.wait_ge(s_sgs[t % 2], 16 * (t // 2))
                            g.activation(sga[t % 2], a[:], ACT.Sigmoid).then_inc(s_taken, 1)
                    if kind == "silu":
                        n, m = it[1], conv_no[it[1]]
                        act.wait_ge(s_taken, n + 1)
                        if m > 2:
                            act.wait_ge(s_cst[m % 2], 16 * ((m - 1) // 2))
                            act.wait_ge(s_sqr, min(m - 2, 2 * NH))
                        g.activation(so[:, m % 2, :], cs[:, m % 2, :], ACT.Silu).then_inc(s_silu, 1)
                    if kind == "gates":
                        act.wait_ge(s_small, 48)
                        act.wait_ge(s_link, 2)
                        g.activation(beta[:], bat[:, 0, :, 0:NH], ACT.Sigmoid).then_inc(s_bact, 1)
                        g.activation(bat[:, 3, :, 0:NH], bat[:, 1, :, 0:NH], ACT.Abs).then_inc(s_bact, 1)
                        act.wait_ge(s_bact, 2)
                        g.activation(bat[:, 4, :, 0:NH], bat[:, 3, :, 0:NH], ACT.Exp, scale=-1.0).then_inc(s_bact, 1)
                        g.activation(bat[:, 3, 0, NH:2 * NH], alog[:], ACT.Exp).then_inc(s_bact, 1)
                        act.wait_ge(s_link, 4)
                        g.activation(bat[:, 5, :, 0:NH], bat[:, 4, :, 0:NH], ACT.Ln).then_inc(s_bact, 1)
                    if kind == "gatesum":
                        act.wait_ge(s_atpe, att_no[it])
                        g.activation(dec[:].rearrange("p a c h -> p (a c h)"), att0[:, 0:3 * NT * NH],
                                     ACT.Exp).then_inc(s_attk, 1)
                    if kind == "dn":
                        name, c = it[1:]
                        if name == "kT":
                            act.wait_ge(s_dn, dn_done[(name, c)])
                            g.activation(X1[:], A4, ACT.Copy).then_inc(s_a, 1)
                        if name == "kkD":
                            act.wait_ge(s_dn, dn_done[(name, c)])
                            g.activation(DTm[:], B4, ACT.Exp).then_inc(s_b, 1)
                        if name == "uw":
                            act.wait_ge(s_dn, dn_done[(name, c)])
                            g.activation(X1[:], A4, ACT.Copy).then_inc(s_a, 1)
                    if kind == "a_qk":
                        grp, i = it[1]
                        nk = P * len(key_tiles(grp, i))
                        act.wait_ge(s_nm, unit_no[it[1]])
                        for q in range(AH):
                            last = g.activation(sc[:, q, 0:nk], sc[:, q, 0:nk], ACT.Exp, bias=mx[:, 1, q:q + 1],
                                                scale=ATT_SCALE)
                        last.then_inc(s_p, 1)
                    if kind == "a_pT":
                        nb = AH * len(key_tiles(*it[1]))
                        act.wait_ge(s_atpe, att_no[it])
                        g.activation(PT[:, 0:nb, :].rearrange("p b c -> p (b c)"), att_ps[:, 0:nb * P],
                                     ACT.Copy).then_inc(s_attk, 1)
                    if kind == "cmb":
                        i = it[1]
                        act.wait_ge(s_cd, i + 1)
                        g.activation(cbs[:, 1], cbs[:, 0], ACT.Exp, scale=ATT_SCALE).then_inc(s_ce, 1)
                        act.wait_ge(s_atpe, att_no[it])
                        if i:
                            act.wait_ge(s_cs, 16 * i)
                        g.activation(oat.rearrange("p a c -> p (a c)"), att0[:, 0:2 * P], ACT.Copy).then_inc(s_attk, 1)

            @block.vector
            def _(dve):
                g = nc.vector
                links = 0

                def link(ins):
                    nonlocal links
                    links += 1
                    ins.then_inc(s_link, 1)
                    dve.wait_ge(s_link, links)

                def variance(c):
                    dve.wait_ge(s_osq, c + 1)
                    link(g.reduce_sum(tiny[:, 0, :], sqo[:], AX))
                    g.tensor_tensor(tiny[:, 1, :], tiny[:, 0, :], rq2[:, :, c], ALU.mult).then_inc(s_ov, 1)
                    dve.wait_ge(s_ov, 2 * c + 1)
                    g.tensor_scalar(tiny[:, 1, :], tiny[:, 1, :], EPS, None, ALU.add).then_inc(s_ov, 1)

                dve.wait_ge(s_masks, 1)
                for it in items:
                    kind = it[0]
                    if kind == "evac" and jobs[it[1]][0] == "conv":
                        n, t = it[1], jobs[it[1]][1]
                        m = conv_no[n]
                        a, c0 = acc[n % 2], cs[:, m % 2, :]
                        dve.wait_ge(s_tap0, m)
                        for j in range(1, CONV):
                            w = PT_DN + (CONV - 1 - j) * 3 * NH + t
                            ins = g.scalar_tensor_tensor(c0[:, j:S], a[:, 0:S - j], prm[:, w:w + 1], c0[:, j:S],
                                                         ALU.mult, ALU.add)
                            if j < CONV - 1:
                                ins.then_inc(s_tap, 1)
                                dve.wait_ge(s_tap, (CONV - 2) * (m - 1) + j)
                            else:
                                ins.then_inc(s_taken, 1)
                    if kind == "rnorm":
                        dve.wait_ge(s_ssq, 2 * NH)
                        g.tensor_scalar(rr[:].rearrange("p a h c -> p (a h c)"), bank_b[:, 0:2 * NH * NT], EPS, None,
                                        ALU.add).then_inc(s_ssum, 1)
                    if kind == "gates":
                        dve.wait_ge(s_small, 48)
                        dve.wait_ge(s_atpe, att_no[it])
                        ins = g.tensor_copy(bat[:, 0].rearrange("p c h -> p (c h)"), att0[:, 0:NT * 2 * NH])
                        link(ins)
                        link(g.tensor_tensor(bat[:, 1, :, 0:NH], bat[:, 0, :, NH:2 * NH],
                                             dtb[:].unsqueeze(1).to_broadcast([P, NT, NH]), ALU.add))
                        link(g.tensor_scalar(bat[:, 2, :, 0:NH], bat[:, 1, :, 0:NH], 0.0, None, ALU.max))
                        dve.wait_ge(s_bact, 4)
                        link(g.tensor_scalar(bat[:, 4, :, 0:NH], bat[:, 4, :, 0:NH], 1.0, None, ALU.add))
                        dve.wait_ge(s_bact, 5)
                        link(g.tensor_tensor(bat[:, 2, :, 0:NH], bat[:, 2, :, 0:NH], bat[:, 5, :, 0:NH], ALU.add))
                        link(g.tensor_scalar(bat[:, 2, :, 0:NH], bat[:, 2, :, 0:NH], -1.0, None, ALU.mult))
                        g.tensor_tensor(g_all[:], bat[:, 2, :, 0:NH],
                                        bat[:, 3, 0, NH:2 * NH].unsqueeze(1).to_broadcast([P, NT, NH]),
                                        ALU.mult).then_inc(s_attk, 1)
                    if kind == "gatesum":
                        dve.wait_ge(s_attk, att_no[it])
                        g.tensor_tensor(bE[:], beta[:], eg, ALU.mult).then_inc(s_gready, 1)
                    if kind == "dn":
                        name, c = it[1:]
                        if name == "kT" and c:
                            variance(c - 1)
                        if name == "ob" and c == NT - 1:
                            variance(c)
                        dve.wait_ge(s_dn, dn_done[(name, c)])
                        if name == "kv":
                            if c == 0:
                                dve.wait_ge(s_rr, 4)
                            g.tensor_tensor(vb[:], B4, bc(beta[:, c, :]), ALU.mult).then_inc(s_b, 1)
                            g.tensor_tensor(kh[:], A4, bc(rr[:, 1, :, c]), ALU.mult).then_inc(s_a, 1)
                        if name == "kkD":
                            dve.wait_ge(s_dtm, c + 1)
                            g.tensor_tensor(WT[:], A4, DTm[:], ALU.mult).then_inc(s_a, 1)
                        if name == "kq":
                            g.tensor_tensor(KQd[:], A4, DTm[:], ALU.mult).then_inc(s_a, 1)
                        if name[0] == "P":
                            g.tensor_tensor(Pb[:], A4, bc(beta[:, c, :]), ALU.mult).then_inc(s_a, 1)
                        if name == "P0":
                            dve.wait_ge(s_a, a_taken[(name, c)])
                            g.tensor_tensor(X1[:], bh(ident[:]), Pb[:], ALU.subtract).then_inc(s_t0, 1)
                        if name == "U0":
                            g.tensor_tensor(Ub[:], bh(ident[:]), B4, ALU.subtract).then_inc(s_b, 1)
                        if name[0] == "T":
                            g.tensor_tensor(Ub[:], Ub[:], B4, ALU.subtract).then_inc(s_b, 1)
                            if (name, c) in a_taken:
                                g.tensor_tensor(X1[:], X1[:], A4, ALU.subtract).then_inc(s_a, 1)
                        if name == "uw":
                            g.tensor_copy(WT[:], B4).then_inc(s_b, 1)
                        if name == "sq":
                            g.tensor_tensor(Pb[:], X1[:], A4, ALU.subtract).then_inc(s_a, 1)
                            if c:
                                dve.wait_ge(s_on, 3 * c)
                            g.tensor_tensor(o1[:], B4, bc(eg[:, c, :]), ALU.mult).then_inc(s_b, 1)
                        if name == "so":
                            dve.wait_ge(s_sd, c + 1)
                            g.tensor_tensor(St[:], DTm[:], A4, ALU.add).then_inc(s_a, 1)
                            dve.wait_ge(s_b, b_taken[("sq", c)])
                            g.tensor_tensor(o1[:], o1[:], B4, ALU.add).then_inc(s_b, 1)
                        if name == "ob":
                            dve.wait_ge(s_ckz, 16 * (c + 1))
                            if c:
                                dve.wait_ge(s_obst, 16 * c)
                            g.scalar_tensor_tensor(obt[:], A4, onw[:, 0:1], ck[:, 3 * NH:4 * NH, :], ALU.mult,
                                                   ALU.mult).then_inc(s_a, 1)
                    if kind == "vT":
                        t = it[1]
                        dve.wait_ge(s_atpe, att_no[it])
                        g.tensor_copy(V[t // 2 % 2][:, :, 2 * (t % 2):2 * (t % 2) + 2, 0:DH],
                                      att_ps[:].rearrange("p (i h c) -> p i h c", i=NT, h=2)).then_inc(s_attk, 1)
                    if kind == "a_qk":
                        grp, i = it[1]
                        u = unit_no[it[1]]
                        nk = P * len(key_tiles(grp, i))
                        mask = dmask[:] if grp == 2 else amask[:, 2 * P - nk:2 * P]
                        dve.wait_ge(s_atpe, att_no[it])
                        g.tensor_tensor(sc[:, :, 0:nk], att4[:, :, 0:nk],
                                        mask.unsqueeze(1).to_broadcast([P, AH, nk]), ALU.add).then_inc(s_attk, 1)
                        dve.wait_ge(s_attk, att_no[it])
                        link(g.reduce_max(mx[:, 0, :], sc[:, :, 0:nk], AX))
                        g.tensor_scalar(mx[:, 1, :], mx[:, 0, :], -ATT_SCALE, None, ALU.mult).then_inc(s_nm, 1)
                    if kind == "a_pv":
                        u = unit_no[it[1]]
                        dve.wait_ge(s_atpe, att_no[it])
                        if u > 1:
                            dve.wait_ge(s_ost, o_stored[att_units()[u - 2]])
                        g.tensor_copy(O[:, :, 0:DH + 1],
                                      att0[:, 0:AH * (DH + 1)].rearrange("p (h c) -> p h c", h=AH)).then_inc(s_attk, 1)
                        g.tensor_copy(O[:, :, DH + 1].rearrange("p (i a) -> p a i", a=2),
                                      mx[:, 0, :].rearrange("p (a i) -> p a i", a=2)).then_inc(s_o, 1)
                    if kind == "cmb":
                        i = it[1]
                        X = cb[i % 2]
                        dve.wait_ge(s_cl[i % 2], 16 * (i // 2 + 1))
                        top = X[:, :, :, DH + 1]
                        link(g.tensor_tensor(cbm[:, 0], top[:, 0], top[:, 1], ALU.max))
                        link(g.tensor_tensor(cbm[:, 1], cbm[:, 0], top[:, 2], ALU.max))
                        g.tensor_tensor(cbs[:, 0], top, cbm[:, 1].unsqueeze(1).to_broadcast([P, NG, AH]),
                                        ALU.subtract).then_inc(s_cd, 1)
                        dve.wait_ge(s_ce, i + 1)
                        link(g.tensor_tensor(cbs[:, 2], cbs[:, 1], X[:, :, :, DH], ALU.mult))
                        link(g.tensor_tensor(cbm[:, 0], cbs[:, 2, 0], cbs[:, 2, 1], ALU.add))
                        link(g.tensor_tensor(cbm[:, 1], cbm[:, 0], cbs[:, 2, 2], ALU.add))
                        link(g.reciprocal(cbm[:, 2], cbm[:, 1]))
                        link(g.tensor_tensor(cbs[:, 3], cbs[:, 1], cbm[:, 2].unsqueeze(1).to_broadcast([P, NG, AH]),
                                             ALU.mult))
                        for q in range(NG):
                            ins = g.tensor_tensor(X[:, q, :, 0:DH], X[:, q, :, 0:DH],
                                                  cbs[:, 3, q].unsqueeze(2).to_broadcast([P, AH, DH]), ALU.mult)
                        link(ins)
                        oc = ocb.rearrange("p (h c) -> p h c", h=AH)
                        if i:
                            dve.wait_ge(s_atpe, att_no[("cmb", i - 1)])
                        link(g.tensor_tensor(oc, X[:, 0, :, 0:DH], X[:, 1, :, 0:DH], ALU.add))
                        g.tensor_tensor(oc, oc, X[:, 2, :, 0:DH], ALU.add).then_inc(s_co, 1)

            @block.tensor
            def _(pe):
                t_ = nc.tensor
                pe.wait_ge(s_masks, 1)

                def each_head(out4, lhs, rhs, transpose=False):
                    for h in range(NH):
                        r = ident[:] if rhs is None else rhs[:, h, :]
                        if transpose:
                            last = t_.transpose(out4[:, h, :], lhs[:, h, :], ident[:])
                        else:
                            last = t_.matmul(out4[:, h, :], lhs[:, h, :], r, start=True, stop=True)
                    return last

                for it in items:
                    kind = it[0]
                    if kind == "mm":
                        n, k = it[1], it[2]
                        if k == 0:
                            pe.wait_ge(s_wlo, n + 1)
                            if n >= 2:
                                pe.wait_ge(s_taken, n - 1)
                        mm = product3(nc, acc[n % 2], wh[:, n % 2, k, :], wl[:, n % 2, k, :], xh[:, k, :], xl[:, k, :],
                                      HALVES, k == 0, k == KT - 1)
                        if k == KT - 1:
                            mm.then_inc(s_acc, 1)
                    if kind == "ssq":
                        t = it[1]
                        pe.wait_ge(s_sqr, t + 1)
                        for c in range(NT):
                            last = t_.matmul(bank_b[:, t * NT + c:t * NT + c + 1], sqb[:, c * P:(c + 1) * P],
                                             ones[:, 0:1], start=True, stop=True)
                        last.then_inc(s_ssq, 1)
                    if it in att_no:
                        if att_no[it] > 1:
                            pe.wait_ge(s_attk, att_no[it] - 1)
                    if kind == "gates":
                        pe.wait_ge(s_taken, 1)
                        for c in range(NT):
                            last = t_.transpose(att0[:, c * 2 * NH:(c + 1) * 2 * NH], bas[0:2 * NH, c * P:(c + 1) * P],
                                                ident[0:2 * NH, 0:2 * NH])
                        last.then_inc(s_atpe, 1)
                    if kind == "gatesum":
                        for j, m in enumerate((U, Ls, ones)):
                            last = t_.matmul(att0[:, j * NT * NH:(j + 1) * NT * NH], m[:],
                                             g_all[:].rearrange("p c h -> p (c h)"), start=True, stop=True)
                        last.then_inc(s_atpe, 1)
                    if kind == "vT":
                        pe.wait_ge(s_taken, job_no[("v", it[1])] + 1)
                        for i in range(NT):
                            last = t_.transpose(att_ps[:, i * P:(i + 1) * P], vt[:, i * P:(i + 1) * P], ident[:])
                        last.then_inc(s_atpe, 1)
                    if kind == "a_qk":
                        grp, i = it[1]
                        tiles = key_tiles(grp, i)
                        keys = slice(tiles[0] * P, (tiles[-1] + 1) * P)
                        for h in (0, 2, 1, 3):
                            rows = slice((h % 2) * DH, (h % 2 + 1) * DH)
                            last = t_.matmul(att4[:, slot(h), 0:P * len(tiles)],
                                             qk[grp % 2][rows, h // 2, i * P:(i + 1) * P],
                                             qk[grp % 2][rows, 2 + h // 2, keys], start=True, stop=True)
                        last.then_inc(s_atpe, 1)
                    if kind == "a_pT":
                        grp, i = it[1]
                        nb = len(key_tiles(grp, i))
                        pe.wait_ge(s_p, unit_no[it[1]])
                        for q in range(AH):
                            for b in range(nb):
                                j = q * nb + b
                                last = t_.transpose(att_ps[:, j * P:(j + 1) * P], sc[:, q, b * P:(b + 1) * P], ident[:])
                        last.then_inc(s_atpe, 1)
                    if kind == "a_pv":
                        grp, i = it[1]
                        tiles = key_tiles(grp, i)
                        for h in range(AH):
                            for b, tile in enumerate(tiles):
                                last = t_.matmul(att0[:, h * (DH + 1):(h + 1) * (DH + 1)],
                                                 PT[:, slot(h) * len(tiles) + b, :], V[grp % 2][:, tile, h, :],
                                                 start=b == 0, stop=b == len(tiles) - 1)
                        last.then_inc(s_atpe, 1)
                    if kind == "cmb":
                        pe.wait_ge(s_co, it[1] + 1)
                        for j in range(2):
                            last = t_.transpose(att0[:, j * P:(j + 1) * P], ocb[:, j * P:(j + 1) * P], ident[:])
                        last.then_inc(s_atpe, 1)
                    if kind == "dn":
                        name, c = it[1:]
                        key = (name, c)
                        if key in a_taken and a_taken[key] > 1:
                            pe.wait_ge(s_a, a_taken[key] - 1)
                        if key in b_taken and b_taken[key] > 1:
                            pe.wait_ge(s_b, b_taken[key] - 1)
                        if name == "kv":
                            if c == 0:
                                pe.wait_ge(s_ssum, 1)
                            pe.wait_ge(s_ckkv, 16 * (c + 1))
                            each_head(A4, ck[:, NH:2 * NH, :], None, True)
                            last = each_head(B4, ck[:, 2 * NH:3 * NH, :], None, True)
                        if name == "kT":
                            last = each_head(A4, kh, None, True)
                        if name == "kkD":
                            pe.wait_ge(s_gu, c + 1)
                            each_head(A4, X1, X1)
                            last = t_.matmul(bank_b[:, :], Ls[:], Pb[:].rearrange("p h c -> p (h c)"), start=True,
                                             stop=True)
                        if name == "kq":
                            pe.wait_ge(s_ckq, 16 * (c + 1))
                            last = each_head(A4, X1, ck[:, 0:NH, :])
                        if name[0] == "P":
                            lv = int(name[1:])
                            pe.wait_ge(s_lm, c * LEVELS + lv + 1)
                            if lv == 1:
                                pe.wait_ge(s_t0, c + 1)
                            last = each_head(A4, Lm[lv % 2], X1 if lv else None)
                        if name == "U0":
                            pe.wait_ge(s_a, a_taken[("P0", c)])
                            last = each_head(B4, Pb, None)
                        if name[0] == "T":
                            pe.wait_ge(s_a, a_taken[("P" + name[1:], c)])
                            if key in a_taken:
                                each_head(A4, Ub, Pb)
                            last = each_head(B4, Pb, Ub)
                        if name == "uw":
                            pe.wait_ge(s_b, b_taken[(f"T{LEVELS - 1}", c)])
                            pe.wait_ge(s_kk, c + 1)
                            each_head(A4, Ub, vb)
                            last = each_head(B4, kbe, Ub)
                        if name == "sq":
                            each_head(A4, WT, St)
                            last = each_head(B4, ck[:, 0:NH, :], St)
                        if name == "so":
                            each_head(A4, kd, Pb)
                            last = each_head(B4, KQd, Pb)
                        if name == "ob":
                            pe.wait_ge(s_on, 3 * (c + 1))
                            last = each_head(A4, on, None, True)
                        last.then_inc(s_dn, 1)


def merge(nc, sem, sb, acc, att_ps, xh, xl, y, w_in2, w_pa2, w_pb2, oa_d, ob_d, sga_d):
    NA, NB = AO // P, DW // P
    NW = KT + NA + NB
    s_o, s_oh, s_ol = sem("g_o_loaded"), sem("g_o_high"), sem("g_o_low")
    s_raw, s_sga = [sem("g_w_loaded0"), sem("g_w_loaded1")], [sem("g_sga_loaded0"), sem("g_sga_loaded1")]
    s_whi, s_wlo = sem("g_w_high"), sem("g_w_low")
    s_pa, s_gb, s_pb = sem("g_pa_done"), sem("g_gate_done"), sem("g_pb_done")
    s_y1, s_sig, s_t, s_y2 = sem("g_first_term"), sem("g_sigmoid"), sem("g_second_term"), sem("g_y_ready")
    with ExitStack() as ctx:
        raw = sb(ctx, "g_raw", [P, 2, NW, P])
        wh = sb(ctx, "g_wh", [P, 2, NW, P], F32R)
        wl = sb(ctx, "g_wl", [P, 2, NW, P], F32R)
        oh = sb(ctx, "g_oh", [P, NA + NB, S], F32R)
        ol = sb(ctx, "g_ol", [P, NA + NB, S], F32R)
        sga = sb(ctx, "g_sga", [P, 2, S])
        sig = sb(ctx, "g_sig", [P, S])
        o_in = y[:, KT - NA - NB:KT, :]
        with nc.Block() as block:

            @block.sync
            def _(sp):
                def load(m):
                    if m >= 2:
                        sp.wait_ge(s_wlo, m - 1)
                    cols = slice(m * P, (m + 1) * P)
                    col = COL_GB + m * P
                    for lo, hi, src in ((0, KT, w_in2[:, col:col + P]), (KT, KT + NA, w_pa2[:, cols]),
                                        (KT + NA, NW, w_pb2[:, cols])):
                        sp.dma_start(raw[:, m % 2, lo:hi, :],
                                     src.rearrange("(k p) c -> p k c", p=P)).then_inc(s_raw[m % 2], 16)
                    if m >= 2:
                        sp.wait_ge(s_y1, m - 1)
                    sp.dma_start(sga[:, m % 2, :], sga_d[m]).then_inc(s_sga[m % 2], 16)

                load(0)
                sp.dma_start(o_in[:, 0:NA, :], oa_d.rearrange("a p c -> p a c")).then_inc(s_o, 16)
                sp.dma_start(o_in[:, NA:NA + NB, :], ob_d.rearrange("a p c -> p a c")).then_inc(s_o, 16)
                for m in range(1, KT):
                    load(m)

            @block.scalar
            def _(act):
                def split(m):
                    act.wait_ge(s_raw[m % 2], 48 * (m // 2 + 1))
                    if m >= 2:
                        act.wait_ge(s_pb, m - 1)
                    nc.scalar.activation(wh[:, m % 2], raw[:, m % 2], ACT.Copy).then_inc(s_whi, 1)

                split(0)
                act.wait_ge(s_o, 32)
                for k in range(NA + NB):
                    nc.scalar.activation(oh[:, k, :], o_in[:, k, :], ACT.Copy).then_inc(s_oh, 1)
                for m in range(KT):
                    if m + 1 < KT:
                        split(m + 1)
                    act.wait_ge(s_gb, m + 1)
                    if m:
                        act.wait_ge(s_y2, m)
                    nc.scalar.activation(sig[:], acc[0][:], ACT.Sigmoid).then_inc(s_sig, 1)

            @block.gpsimd
            def _(pool):
                for m in range(KT):
                    pool.wait_ge(s_whi, m + 1)
                    nc.gpsimd.tensor_tensor(wl[:, m % 2], raw[:, m % 2], wh[:, m % 2].bitcast(F32),
                                            ALU.subtract).then_inc(s_wlo, 1)

            @block.vector
            def _(dve):
                for k in range(NA + NB):
                    dve.wait_ge(s_oh, k + 1)
                    nc.vector.tensor_tensor(ol[:, k, :], o_in[:, k, :], oh[:, k, :].bitcast(F32),
                                            ALU.subtract).then_inc(s_ol, 1)
                for m in range(KT):
                    dve.wait_ge(s_pa, m + 1)
                    dve.wait_ge(s_sga[m % 2], 16 * (m // 2 + 1))
                    if m == KT - NA - NB:
                        dve.wait_ge(s_ol, NA + NB)
                    nc.vector.tensor_tensor(y[:, m, :], sga[:, m % 2, :], acc[1][:], ALU.mult).then_inc(s_y1, 1)
                    dve.wait_ge(s_pb, m + 1)
                    dve.wait_ge(s_sig, m + 1)
                    nc.vector.tensor_tensor(sig[:], sig[:], att_ps[:], ALU.mult).then_inc(s_t, 1)
                    dve.wait_ge(s_t, m + 1)
                    nc.vector.tensor_tensor(y[:, m, :], y[:, m, :], sig[:], ALU.add).then_inc(s_y2, 1)

            @block.tensor
            def _(pe):
                def rows(out, m, w0, n, high, low):
                    for k in range(n):
                        mm = product3(nc, out, wh[:, m % 2, w0 + k, :], wl[:, m % 2, w0 + k, :], high[:, k, :],
                                      low[:, k, :], HALVES, k == 0, k == n - 1)
                    return mm

                for m in range(KT):
                    pe.wait_ge(s_wlo, m + 1)
                    if m:
                        pe.wait_ge(s_sig, m)
                    rows(acc[0], m, 0, KT, xh, xl).then_inc(s_gb, 1)
                    if m == 0:
                        pe.wait_ge(s_ol, NA + NB)
                    else:
                        pe.wait_ge(s_y1, m)
                    rows(acc[1], m, KT, NA, oh, ol).then_inc(s_pa, 1)
                    if m:
                        pe.wait_ge(s_t, m)
                    rows(att_ps, m, KT + NA, NB, oh[:, NA:NA + NB, :], ol[:, NA:NA + NB, :]).then_inc(s_pb, 1)


def project_out(nc, sem, sb, every, ident, prm, small, xh, xl, y, w_o2, xd, h_d):
    ss, ms, rstd, mhalf = small[:, 0:8], small[:, 8:16], small[:, 16:24], small[:, 24:32]
    NQ = 4
    QC = D // NQ
    NBK = 4
    s_yh, s_yl, s_x = sem("p_y_high"), sem("p_y_low"), sem("p_x_loaded")
    s_raw, s_whi, s_wlo = sem("p_w_loaded"), sem("p_w_high"), sem("p_w_low")
    s_mm, s_h = sem("p_product"), sem("p_h_added")
    s_sq, s_ms, s_rstd, s_xn = sem("p_squares"), sem("p_mean_square"), sem("p_rstd"), sem("p_scaled")
    s_tr, s_f, s_hi, s_lo, s_st = (sem("p_transposed"), sem("p_weighted"), sem("p_high"), sem("p_low"),
                                   sem("p_h_stored"))
    with ExitStack() as ctx:
        yh = sb(ctx, "yh", [P, KT, S], F32R)
        yl = sb(ctx, "yl", [P, KT, S], F32R)
        raw = sb(ctx, "p_raw", [P, KT, QC])
        wh = sb(ctx, "p_wh", [P, KT, QC], F32R)
        wl = sb(ctx, "p_wl", [P, KT, QC], F32R)
        xn = sb(ctx, "p_xn", [P, D])
        xf = sb(ctx, "p_xf", [P, KT, P])
        junk = sb(ctx, "p_junk", [P, D])
        h = y
        t2 = [[every[4], every[5]], [every[6], every[7]]]
        with nc.Block() as block:

            @block.sync
            def _(sp):
                def load_w(q):
                    if q:
                        sp.wait_ge(s_wlo, q)
                    sp.dma_start(raw[:], w_o2[:, q * QC:(q + 1) * QC].rearrange("(k p) c -> p k c", p=P)
                                 ).then_inc(s_raw, 16)

                load_w(0)
                for st in range(NT):
                    sp.wait_ge(s_yl, st + 1)
                    sp.dma_start(h[:, st, :], xd[st * P:(st + 1) * P, :]).then_inc(s_x, 16)
                for q in range(1, NQ):
                    load_w(q)
                for st in range(NT):
                    sp.wait_ge(s_h, (NQ - 1) * NT + st + 1)
                    sp.dma_start(h_d[st * P:(st + 1) * P, :], h[:, st, :]).then_inc(s_st, 16)
                sp.wait_ge(s_st, 16 * NT)

            @block.scalar
            def _(act):
                for k in range(KT):
                    if k == 1:
                        act.wait_ge(s_raw, 16)
                        nc.scalar.activation(wh[:], raw[:], ACT.Copy).then_inc(s_whi, 1)
                    nc.scalar.activation(yh[:, k, :], y[:, k, :], ACT.Copy).then_inc(s_yh, 1)
                for q in range(1, NQ):
                    act.wait_ge(s_raw, 16 * (q + 1))
                    act.wait_ge(s_mm, q * NT)
                    nc.scalar.activation(wh[:], raw[:], ACT.Copy).then_inc(s_whi, 1)
                for st in range(NT + 1):
                    if st < NT:
                        act.wait_ge(s_h, (NQ - 1) * NT + st + 1)
                        if st:
                            act.wait_ge(s_sq, st)
                        nc.scalar.activation(junk[:], h[:, st, :], ACT.Square,
                                             accum_out=ss[:, st:st + 1]).then_inc(s_sq, 1)
                    if st:
                        act.wait_ge(s_f, 2 * st)
                        nc.scalar.activation(xh[:, :, (st - 1) * P:st * P], xf[:], ACT.Copy).then_inc(s_hi, 1)

            @block.gpsimd
            def _(pool):
                for q in range(NQ):
                    pool.wait_ge(s_whi, q + 1)
                    nc.gpsimd.tensor_tensor(wl[:], raw[:], wh[:].bitcast(F32), ALU.subtract).then_inc(s_wlo, 1)
                for st in range(NT + 1):
                    if st < NT:
                        pool.wait_ge(s_ms, st + 1)
                        nc.gpsimd.tensor_tensor(rstd[:, st:st + 1], ms[:, st:st + 1], mhalf[:, 0:1],
                                                ALU.pow).then_inc(s_rstd, 1)
                    if st:
                        pool.wait_ge(s_hi, st)
                        cols = slice((st - 1) * P, st * P)
                        nc.gpsimd.tensor_tensor(xl[:, :, cols], xf[:], xh[:, :, cols].bitcast(F32),
                                                ALU.subtract).then_inc(s_lo, 1)

            @block.vector
            def _(dve):
                for k in range(KT):
                    dve.wait_ge(s_yh, k + 1)
                    nc.vector.tensor_tensor(yl[:, k, :], y[:, k, :], yh[:, k, :].bitcast(F32),
                                            ALU.subtract).then_inc(s_yl, 1)
                dve.wait_ge(s_x, 16 * NT)

                def weigh(st):
                    dve.wait_ge(s_tr, st + 1)
                    if st:
                        dve.wait_ge(s_lo, st)
                    for j in range(2):
                        w = prm[:, PT_N2 + 4 * j:PT_N2 + 4 * j + 4].unsqueeze(2).to_broadcast([P, 4, P])
                        nc.vector.tensor_tensor(xf[:, 4 * j:4 * j + 4, :],
                                                t2[st % 2][j].rearrange("p (k c) -> p k c", k=4), w,
                                                ALU.mult).then_inc(s_f, 1)

                for q in range(NQ):
                    for st in range(NT):
                        n = q * NT + st
                        dve.wait_ge(s_mm, n + 1)
                        cols = slice(q * QC, (q + 1) * QC)
                        nc.vector.tensor_tensor(h[:, st, cols], h[:, st, cols], every[n % NBK][:, 0:QC],
                                                ALU.add).then_inc(s_h, 1)
                        if q == NQ - 1:
                            if st:
                                weigh(st - 1)
                            dve.wait_ge(s_sq, st + 1)
                            nc.vector.tensor_scalar(ms[:, st:st + 1], ss[:, st:st + 1], 1.0 / D, EPS, ALU.mult,
                                                    ALU.add).then_inc(s_ms, 1)
                            dve.wait_ge(s_rstd, st + 1)
                            if st:
                                dve.wait_ge(s_tr, st)
                            nc.vector.tensor_scalar(xn[:], h[:, st, :], rstd[:, st:st + 1], None,
                                                    ALU.mult).then_inc(s_xn, 1)
                weigh(NT - 1)

            @block.tensor
            def _(pe):
                def transposes(st):
                    pe.wait_ge(s_xn, st + 1)
                    if st >= 2:
                        pe.wait_ge(s_f, 2 * (st - 1))
                    for k in range(KT):
                        last = nc.tensor.transpose(t2[st % 2][k // 4][:, (k % 4) * P:(k % 4 + 1) * P],
                                                   xn[:, k * P:(k + 1) * P], ident[:])
                    last.then_inc(s_tr, 1)

                for q in range(NQ):
                    pe.wait_ge(s_wlo, q + 1)
                    for st in range(NT):
                        n = q * NT + st
                        if n >= NBK:
                            pe.wait_ge(s_h, n - NBK + 1)
                        rows = slice(st * P, (st + 1) * P)
                        for k in range(KT):
                            if n == 0:
                                pe.wait_ge(s_yl, k + 1)
                            for j, (a, b) in enumerate(((yh, wh), (yh, wl), (yl, wh))):
                                mm = nc.tensor.matmul(every[n % NBK][:, 0:QC], a[:, k, rows], b[:, k, :],
                                                      start=k == 0 and j == 0, stop=k == KT - 1 and j == 2)
                        mm.then_inc(s_mm, 1)
                        if q == NQ - 1 and st >= 2:
                            transposes(st - 2)
                transposes(NT - 2)
                transposes(NT - 1)


def ffn(nc, sem, sb, acc, every, prm, small, xh, xl, w_up2, w_dn2, h_d, final_norm_w, outd):
    with ExitStack() as ctx:
        glu = sb(ctx, "glu", [P, FT, S])
        ffn_up(nc, sem, sb, acc, prm, xh, xl, glu, w_up2)
        ffn_down(nc, sem, sb, every, small, xh, xl, glu, w_dn2, h_d, final_norm_w, outd)


def ffn_up(nc, sem, sb, acc, prm, xh, xl, glu, w_up2):
    s_raw = [sem("u_w_loaded0"), sem("u_w_loaded1")]
    s_whi, s_wlo, s_acc, s_tap0, s_tap, s_taken = (sem("u_w_high"), sem("u_w_low"), sem("u_acc_done"),
                                                   sem("u_tap0"), sem("u_tap1"), sem("u_acc_taken"))
    s_silu, s_glu = sem("u_silu"), sem("u_glu")
    with ExitStack() as ctx:
        raw = sb(ctx, "u_raw", [P, 2, KT, P])
        wh = sb(ctx, "u_wh", [P, 2, KT, P], F32R)
        wl = sb(ctx, "u_wl", [P, 2, KT, P], F32R)
        cv = sb(ctx, "u_conv", [P, 2, S])
        sg = sb(ctx, "u_silu", [P, S])
        with nc.Block() as block:

            @block.sync
            def _(sp):
                def turn(i, first=False):
                    for j in range(2):
                        if not first:
                            sp.wait_ge(s_wlo, 2 * i - 1 + j)
                        src = w_up2[:, bass.ds(i * P + j * FF, P)]
                        sp.dma_start(raw[:, j], src.rearrange("(k p) c -> p k c", p=P)).then_inc(s_raw[j], 16)

                turn(0, True)
                with sp.Fori(1, FT) as i:
                    turn(i)

            @block.scalar
            def _(act):
                def split(i, j, first=False):
                    act.wait_ge(s_raw[j], 16 * i + 16)
                    if not first:
                        act.wait_ge(s_acc, 2 * i - 1 + j)
                    nc.scalar.activation(wh[:, j], raw[:, j], ACT.Copy).then_inc(s_whi, 1)

                def turn(i, first=False, last=False):
                    split(i, 1, first)
                    for j in range(2):
                        act.wait_ge(s_acc, 2 * i + 1 + j)
                        if not first:
                            act.wait_ge(s_glu if j else s_silu, i)
                        w = PT_FFN + (FCONV - 1) * 2 * FT + j * FT
                        b = PT_BIAS + j * FT
                        nc.scalar.activation(cv[:, j, :], acc[j][:], ACT.Identity, bias=prm[:, bass.ds(b + i, 1)],
                                             scale=prm[:, bass.ds(w + i, 1)]).then_inc(s_tap0, 1)
                        if j == 0:
                            if not last:
                                split(i + 1, 0)
                            act.wait_ge(s_taken, 2 * i + 1)
                            if not first:
                                act.wait_ge(s_glu, i)
                            nc.scalar.activation(sg[:], cv[:, 0, :], ACT.Silu).then_inc(s_silu, 1)

                split(0, 0, True)
                turn(0, True)
                with act.Fori(1, FT - 1) as i:
                    turn(i)
                turn(FT - 1, last=True)

            @block.gpsimd
            def _(pool):
                def turn(i):
                    for j in range(2):
                        pool.wait_ge(s_whi, 2 * i + 1 + j)
                        nc.gpsimd.tensor_tensor(wl[:, j], raw[:, j], wh[:, j].bitcast(F32),
                                                ALU.subtract).then_inc(s_wlo, 1)

                with pool.Fori(0, FT) as i:
                    turn(i)

            @block.vector
            def _(dve):
                def turn(i):
                    for j in range(2):
                        dve.wait_ge(s_tap0, 2 * i + 1 + j)
                        for tap in (1, 2):
                            w = PT_FFN + (FCONV - 1 - tap) * 2 * FT + j * FT
                            ins = nc.vector.scalar_tensor_tensor(cv[:, j, tap:S], acc[j][:, 0:S - tap],
                                                                 prm[:, bass.ds(w + i, 1)], cv[:, j, tap:S],
                                                                 ALU.mult, ALU.add)
                            if tap == 1:
                                ins.then_inc(s_tap, 1)
                                dve.wait_ge(s_tap, 2 * i + 1 + j)
                            else:
                                ins.then_inc(s_taken, 1)
                    dve.wait_ge(s_taken, 2 * i + 2)
                    dve.wait_ge(s_silu, i + 1)
                    nc.vector.tensor_tensor(glu[:, bass.ds(i, 1), :], sg[:].unsqueeze(1), cv[:, 1:2, :],
                                            ALU.mult).then_inc(s_glu, 1)

                with dve.Fori(0, FT) as i:
                    turn(i)

            @block.tensor
            def _(pe):
                def turn(i, first=False):
                    for j in range(2):
                        pe.wait_ge(s_wlo, 2 * i + 1 + j)
                        if not first:
                            pe.wait_ge(s_taken, 2 * i - 1 + j)
                        for k in range(KT):
                            mm = product3(nc, acc[j], wh[:, j, k, :], wl[:, j, k, :], xh[:, k, :], xl[:, k, :],
                                          HALVES, k == 0, k == KT - 1)
                        mm.then_inc(s_acc, 1)

                turn(0, True)
                with pe.Fori(1, FT) as i:
                    turn(i)


def ffn_down(nc, sem, sb, every, small, xh, xl, glu, w_dn2, h_d, final_norm_w, outd):
    ss, ms, rstd, mhalf = small[:, 0:8], small[:, 8:16], small[:, 16:24], small[:, 24:32]
    NHALF = D // HALF
    s_raw = [sem("f_w_loaded0"), sem("f_w_loaded1")]
    s_gh, s_gl, s_whi, s_wlo = sem("f_glu_high"), sem("f_glu_low"), sem("f_w_high"), sem("f_w_low")
    s_k, s_bank, s_sum = sem("f_k_done"), sem("f_bank_done"), sem("f_summed")
    s_h, s_fw = sem("f_h_loaded"), sem("f_norm_loaded")
    s_sq, s_ms, s_rstd, s_y, s_out = (sem("f_squares"), sem("f_mean_square"), sem("f_rstd"), sem("f_scaled"),
                                      sem("f_out_stored"))
    with ExitStack() as ctx:
        raw = sb(ctx, "f_raw", [P, 2, HALF])
        h = sb(ctx, "f_h", [P, NT, D])
        fw = sb(ctx, "f_fw", [P, D])
        gh, gl = [xh[:, j, :] for j in range(2)], [xl[:, j, :] for j in range(2)]
        wh, wl = [xh[:, 2 + j, 0:HALF] for j in range(2)], [xl[:, 2 + j, 0:HALF] for j in range(2)]
        junk = [glu[:, j, :] for j in range(2)]
        with nc.Block() as block:
            NQ = FT // 2

            @block.sync
            def _(sp):
                def load(half, q, first=False):
                    for j in range(2):
                        if not first:
                            sp.wait_ge(s_wlo, half * FT + 2 * q - 1 + j)
                        sp.dma_start(raw[:, j, :], w_dn2[bass.ds((2 * q + j) * P, P), half * HALF:(half + 1) * HALF]
                                     ).then_inc(s_raw[j], 16)

                load(0, 0, True)
                for st in range(NT):
                    sp.dma_start(h[:, st, :], h_d[st * P:(st + 1) * P, :]).then_inc(s_h, 16)
                sp.dma_start(fw[:], final_norm_w.unsqueeze(0).to_broadcast([P, D])).then_inc(s_fw, 16)
                with sp.Fori(1, NQ) as q:
                    load(0, q)
                with sp.Fori(0, NQ) as q:
                    load(1, q)
                for st in range(NT):
                    sp.wait_ge(s_y, st + 1)
                    sp.dma_start(outd[st * P:(st + 1) * P, :], h[:, st, :]).then_inc(s_out, 16)
                sp.wait_ge(s_out, 16 * NT)

            @block.scalar
            def _(act):
                def turn(half, q, first=False):
                    for j in range(2):
                        kk = half * FT + 2 * q + j
                        if not first:
                            act.wait_ge(s_k, kk - 1)
                        nc.scalar.activation(gh[j].unsqueeze(1), glu[:, bass.ds(2 * q + j, 1), :],
                                             ACT.Copy).then_inc(s_gh, 1)
                        act.wait_ge(s_raw[j], (half * NQ + q) * 16 + 16)
                        nc.scalar.activation(wh[j], raw[:, j, :], ACT.Copy).then_inc(s_whi, 1)

                turn(0, 0, True)
                with act.Fori(1, NQ) as q:
                    turn(0, q)
                with act.Fori(0, NQ) as q:
                    turn(1, q)
                for st in range(NT):
                    act.wait_ge(s_sum, NT + st + 1)
                    if st:
                        act.wait_ge(s_sq, st)
                    nc.scalar.activation(junk[0], h[:, st, :], ACT.Square, accum_out=ss[:, st:st + 1]).then_inc(s_sq, 1)

            @block.gpsimd
            def _(pool):
                def turn(half, q):
                    for j in range(2):
                        pool.wait_ge(s_gh, half * FT + 2 * q + j + 1)
                        nc.gpsimd.tensor_tensor(gl[j].unsqueeze(1), glu[:, bass.ds(2 * q + j, 1), :],
                                                gh[j].bitcast(F32).unsqueeze(1), ALU.subtract).then_inc(s_gl, 1)

                for half in range(NHALF):
                    with pool.Fori(0, NQ) as q:
                        turn(half, q)
                for st in range(NT):
                    pool.wait_ge(s_ms, st + 1)
                    nc.gpsimd.tensor_tensor(rstd[:, st:st + 1], ms[:, st:st + 1], mhalf[:, 0:1],
                                            ALU.pow).then_inc(s_rstd, 1)

            @block.vector
            def _(dve):
                def low(half, q, j):
                    dve.wait_ge(s_whi, half * FT + 2 * q + j + 1)
                    nc.vector.tensor_tensor(wl[j], raw[:, j, :], wh[j].bitcast(F32), ALU.subtract).then_inc(s_wlo, 1)

                def sums(half):
                    for st in range(NT):
                        dve.wait_ge(s_bank, half * NT + st + 1)
                        cols = slice(half * HALF, (half + 1) * HALF)
                        nc.vector.tensor_tensor(h[:, st, cols], h[:, st, cols], every[st], ALU.add).then_inc(s_sum, 1)
                        if half:
                            norm(st)

                def norm(st):
                    dve.wait_ge(s_sq, st + 1)
                    nc.vector.tensor_scalar(ms[:, st:st + 1], ss[:, st:st + 1], 1.0 / D, EPS, ALU.mult,
                                            ALU.add).then_inc(s_ms, 1)
                    dve.wait_ge(s_rstd, st + 1)
                    nc.vector.scalar_tensor_tensor(h[:, st, :], h[:, st, :], rstd[:, st:st + 1], fw[:], ALU.mult,
                                                   ALU.mult).then_inc(s_y, 1)

                with dve.Fori(0, NQ) as q:
                    low(0, q, 0)
                    low(0, q, 1)
                dve.wait_ge(s_h, 16 * NT)
                dve.wait_ge(s_fw, 16)
                low(1, 0, 0)
                sums(0)
                low(1, 0, 1)
                with dve.Fori(1, NQ) as q:
                    low(1, q, 0)
                    low(1, q, 1)
                sums(1)

            @block.tensor
            def _(pe):
                def turn(half, q, first=False, last=False):
                    for j in range(2):
                        kk = half * FT + 2 * q + j
                        pe.wait_ge(s_gl, kk + 1)
                        pe.wait_ge(s_wlo, kk + 1)
                        for st in range(NT):
                            if first and j == 0 and half:
                                pe.wait_ge(s_sum, st + 1)
                            rows = slice(st * P, (st + 1) * P)
                            for n, (a, b) in enumerate(((gh, wh), (gh, wl), (gl, wh))):
                                mm = nc.tensor.matmul(every[st], a[j][:, rows], b[j], start=first and j == 0 and n == 0,
                                                      stop=last and j == 1 and n == 2)
                            if last and j == 1:
                                mm.then_inc(s_bank, 1)
                        if not (last and j == 1):
                            mm.then_inc(s_k, 1)

                for half in range(NHALF):
                    turn(half, 0, first=True)
                    with pe.Fori(1, NQ - 1) as q:
                        turn(half, q)
                    turn(half, NQ - 1, last=True)


_OUTS = [((1, S, D), "float32")]
_INS = ["x", "norm1_w", "w_in", "dn_conv_w", "dn_a_log", "dn_dt_bias", "dn_onorm_w", "w_pa", "w_pb", "w_o",
        "norm2_w", "w_up", "ffn_conv_w", "ffn_conv_b", "w_down", "final_norm_w"]


def kernel(**inputs):
    import numpy as _np
    import concourse.bacc as _bacc
    from concourse import mybir as _mybir
    from concourse.bass_utils import run_bass_kernel_spmd as _run

    nc = _bacc.Bacc("TRN2", target_bir_lowering=False, num_devices=1)
    arrays, args = {}, []
    for name in _INS:
        a = _np.ascontiguousarray(inputs[name])
        arrays[f"in_{name}_dram"] = a
        args.append(nc.dram_tensor(f"in_{name}_dram", a.shape, _mybir.dt.from_np(a.dtype), kind="ExternalInput").ap())
    for i, (shape, dtype) in enumerate(_OUTS):
        dt = _mybir.dt.from_np(_np.dtype(dtype))
        args.append(nc.dram_tensor(f"out_{i}_dram", shape, dt, kind="ExternalOutput").ap())
    build(nc, *args)
    r = _run(nc, [arrays], core_ids=[0])
    return r.results[0]["out_0_dram"]
```

```python
from contextlib import ExitStack

import concourse.bass as bass
from concourse import mybir

F32 = mybir.dt.float32
F32R = mybir.dt.float32r
ALU = mybir.AluOpType
ACT = mybir.ActivationFunctionType
AX = mybir.AxisListType.X

P = 128
S = 1024
D = 1024
NT = S // P
KT = D // P
HALF = 512
EPS = 1e-6

DH = 64
AH = 4
GROUPS = ((128, 1), (512, 4), (2048, 16))
NG = len(GROUPS)
AW = NG * AH * DH
AO = AH * DH
OC = DH + 2
ATT_SCALE = DH ** -0.5
NEG = -1.0e30

NH = 4
DK = 128
DW = NH * DK
CONV = 4
LEVELS = 7

NBR = (AO + DW) // P

FF = 2816
FT = FF // P
FCONV = 3

COL_Q, COL_K, COL_V = 0, AW, 2 * AW
COL_DN = 3 * AW
COL_BA = COL_DN + 3 * DW
COL_Z = COL_BA + 2 * NH
COL_GATE = COL_Z + DW

PT_FFN = 0
PT_BIAS = FCONV * 2 * FT
PT_DN = PT_BIAS + 2 * FT
PT_N1 = PT_DN + CONV * 3 * NH
PT_N2 = PT_N1 + KT
PT_COLS = PT_N2 + KT


def mixer_jobs():
    jobs = [("ba", 0, COL_BA)]
    jobs += [("conv", t, COL_DN + t * P) for t in range(3 * NH)]
    jobs += [("z", t, COL_Z + t * P) for t in range(NH)]
    for g in range(NG):
        for kind, col in (("q", COL_Q), ("k", COL_K), ("v", COL_V)):
            jobs += [(kind, 2 * g + t, col + (2 * g + t) * P) for t in range(2)]
    jobs += [("gate", t, COL_GATE + t * P) for t in range(2 * KT)]
    return jobs


def dn_stages():
    out = []
    for c in range(NT):
        seq = ["kv", "kT", "kkD", "kq", "P0", "U0"]
        for lv in range(1, LEVELS):
            seq += [f"P{lv}", f"T{lv}"]
        seq += ["uw", "sq", "so"]
        seq = [(name, c) for name in seq]
        if c:
            seq.insert(4, ("ob", c - 1))
        out += seq
    return out + [("ob", NT - 1)]


def att_units():
    return [(g, i) for g in range(NG) for i in range(NT)]


def mixer_schedule(jobs):
    dn = dn_stages()
    items = [("w", 0)]
    ready = []
    units = att_units()
    combine = [(name, i) for i in range(NT) for name in ("cmb", "cmbT")]
    free_slot = 3
    GAP = {"a_qk": 3, "a_pT": 2, "a_pv": 1, "cmb": 4, "cmbT": 4}
    for n, (kind, t, _) in enumerate(jobs):
        for k in range(KT):
            items.append(("mm", n, k))
            if k == 0:
                items.append(("w", n + 1))
            if n and k == 2:
                pk, pt, _ = jobs[n - 1]
                if pk == "ba":
                    items.append(("gates",))
                if pk == "conv":
                    items.append(("silu", n - 1))
                if pk == "v":
                    items.append(("vT", pt))
                    if pt % 2:
                        g = pt // 2
                        for u in units:
                            if u[0] == g:
                                ready += [("a_qk", u), ("a_pT", u), ("a_pv", u)]
            if n and k == 6 and jobs[n - 1][0] == "ba":
                items.append(("gatesum",))
            if n and k == 6 and jobs[n - 1][0] == "conv" and jobs[n - 1][1] < 2 * NH:
                items.append(("ssq", jobs[n - 1][1]))
            if kind == "conv" and t == 2 * NH + 1 and k == 4:
                items.append(("rnorm",))
            if n > 1 + 3 * NH and dn:
                items.append(("dn",) + dn.pop(0))
            slot = t * KT + k
            if kind != "gate" and ready and k % 2 == 0:
                items.append(ready.pop(0))
            elif kind == "gate" and slot >= free_slot and (ready or combine):
                items.append((ready or combine).pop(0))
                free_slot = slot + GAP[items[-1][0]] + (4 if items[-1] == ("a_pv", units[-1]) else 0)
        items.append(("evac", n))
    assert not dn and not ready
    return items + [("w", len(jobs) + 1)] + combine


def count(seq):
    return {key: n + 1 for n, key in enumerate(seq)}


def build(nc, x, norm1_w, w_in, dn_conv_w, dn_a_log, dn_dt_bias, dn_onorm_w, w_pa, w_pb, w_o,
          norm2_w, w_up, ffn_conv_w, ffn_conv_b, w_down, final_norm_w, out):
    xd = x[0]
    outd = out[0]
    w_in2, w_pa2, w_pb2, w_o2, w_up2, w_dn2 = w_in[0], w_pa[0], w_pb[0], w_o[0], w_up[0], w_down[0]
    conv_d = nc.dram_tensor("conv_d", [4 * NH, P, S], F32, kind="Internal").ap()
    og_d = nc.dram_tensor("og_d", [NG, S, AH * OC], F32, kind="Internal").ap()
    oa_d = nc.dram_tensor("oa_d", [2, P, S], F32, kind="Internal").ap()
    ob_d = nc.dram_tensor("ob_d", [NH, P, S], F32, kind="Internal").ap()
    gate_d = nc.dram_tensor("gate_d", [2 * KT, P, S], F32, kind="Internal").ap()
    h_d = nc.dram_tensor("h_d", [S, D], F32, kind="Internal").ap()

    with ExitStack() as top:
        top.enter_context(nc.allow_non_contiguous_dma(reason="a few small parameter rows"))

        def sem(name):
            return top.enter_context(nc.semaphore(name))

        def psum(name, cols=HALF):
            return top.enter_context(nc.psum_tensor(name, [P, cols], F32))

        def sb(ctx, name, shape, dt=F32):
            return ctx.enter_context(nc.sbuf_tensor(name, shape, dt))

        acc = [psum("acc0", S), psum("acc1", S)]
        bank_a, bank_b = psum("bank_a"), psum("bank_b")
        att_ps = psum("att_ps", S)
        every = [acc[0][:, 0:HALF], acc[0][:, HALF:S], acc[1][:, 0:HALF], acc[1][:, HALF:S],
                 bank_a[:, :], bank_b[:, :], att_ps[:, 0:HALF], att_ps[:, HALF:S]]

        ident = sb(top, "ident", [P, P])
        ones = sb(top, "ones", [P, P])
        prm = sb(top, "prm", [P, PT_COLS])
        small = sb(top, "small", [P, 32])
        xh = sb(top, "xh", [P, KT, S], F32R)
        xl = sb(top, "xl", [P, KT, S], F32R)
        ring = (sb(top, "w_raw", [P, 2, KT, P]), sb(top, "w_high", [P, 2, KT, P], F32R),
                sb(top, "w_low", [P, 2, KT, P], F32R))

        def ring_sems(phase):
            return ([sem(f"{phase}_w_loaded{j}") for j in range(2)], sem(f"{phase}_w_high"), sem(f"{phase}_w_low"))

        m_ring, g_ring, u_ring, f_ring = (ring_sems(phase) for phase in "mguf")
        norm_in(nc, sem, sb, every, xd, norm1_w, norm2_w, dn_conv_w, ffn_conv_w, ffn_conv_b,
                ident, ones, prm, small, xh, xl, w_in2, ring, m_ring)
        mixer(nc, sem, sb, acc, bank_a, bank_b, att_ps, ident, ones, prm, xh, xl,
              w_in2, dn_a_log, dn_dt_bias, dn_onorm_w, conv_d, og_d, oa_d, ob_d, gate_d,
              w_pa2, w_pb2, ring, m_ring, g_ring)
        merge_and_project(nc, sem, sb, acc, every, ident, small, prm, xh, xl, w_pa2, w_pb2, w_o2, oa_d, ob_d,
                          gate_d, xd, h_d, w_up2, ring, g_ring, u_ring)
        ffn(nc, sem, sb, acc, every, prm, small, xh, xl, w_up2, w_dn2, h_d, final_norm_w, outd, ring, u_ring, f_ring)


def load_columns(eng, raw, src, loaded):
    eng.dma_start(raw, src.rearrange("(k p) c -> p k c", p=P)).then_inc(loaded, 16)


def load_branch_columns(eng, raw, m, w_pa2, w_pb2, loaded):
    cols = slice(m * P, (m + 1) * P)
    load_columns(eng, raw[:, 0:AO // P, :], w_pa2[:, cols], loaded)
    load_columns(eng, raw[:, AO // P:NBR, :], w_pb2[:, cols], loaded)


def norm_in(nc, sem, sb, every, xd, norm1_w, norm2_w, dn_conv_w, ffn_conv_w, ffn_conv_b,
            ident, ones, prm, small, xh, xl, w_in2, ring, m_ring):
    ss, ms, rstd, mhalf = small[:, 0:8], small[:, 8:16], small[:, 16:24], small[:, 24:32]
    raw, wh, wl = ring
    m_raw, m_whi, m_wlo = m_ring
    first_cols = [job[2] for job in mixer_jobs()[0:2]]
    AHEAD = 4
    s_x, s_par = [sem(f"n_x_loaded{j}") for j in range(AHEAD)], sem("n_params_loaded")
    s_id, s_const = sem("n_const_step"), sem("n_constants_ready")
    s_sq, s_ms, s_rstd, s_xn = sem("n_squares"), sem("n_mean_square"), sem("n_rstd"), sem("n_scaled")
    s_tr, s_f, s_hi, s_lo, s_prm, s_prt = (sem("n_transposed"), sem("n_weighted"), sem("n_high"), sem("n_low"),
                                           sem("n_params_ready"), sem("n_params_transposed"))
    with ExitStack() as ctx:
        xs = sb(ctx, "xs", [P, NT, D])
        junk = sb(ctx, "junk", [P, D])
        xn = sb(ctx, "n_xn", [P, 2, D])
        xf = sb(ctx, "n_xf", [P, 2, KT, P])
        t2 = [[every[0], every[1]], [every[2], every[3]]]
        rows = 2 * FT
        stage = sb(ctx, "stage", [rows, 10, P])
        table = [(PT_FFN + j * rows, rows, j) for j in range(FCONV)] + [(PT_BIAS, rows, FCONV)]
        table += [(PT_DN + j * 3 * NH, 3 * NH, 4 + j) for j in range(CONV)]
        table += [(PT_N1, KT, 8), (PT_N2, KT, 9)]
        params = [ffn_conv_w[0, j] for j in range(FCONV)] + [ffn_conv_b[0]]
        params += [dn_conv_w[0, j] for j in range(CONV)] + [norm1_w[0], norm2_w[0]]

        def load_params(eng, part):
            half = len(params) // 2
            for j in range(part * half, part * half + half):
                m = table[j][1]
                eng.dma_start(stage[0:m, j, :], params[j].rearrange("(m p) -> m p", p=P)).then_inc(s_par, 16)

        with nc.Block() as block:

            @block.sync
            def _(sp):
                for i in range(NT):
                    if i == AHEAD:
                        load_params(sp, 1)
                    if i >= AHEAD:
                        sp.wait_ge(s_x[i % AHEAD], 16 * (i // AHEAD))
                    sp.dma_start(xs[:, i, :], xd[i * P:(i + 1) * P, :]).then_inc(s_x[i % AHEAD], 16)
                for n in range(2):
                    load_columns(sp, raw[:, n], w_in2[:, first_cols[n]:first_cols[n] + P], m_raw[n])

            @block.scalar
            def _(act):
                load_params(act, 0)

                def square(i):
                    act.wait_ge(s_x[i % AHEAD], 16 * (i // AHEAD + 1))
                    if i:
                        act.wait_ge(s_sq, i)
                    nc.scalar.activation(junk[:], xs[:, i, :], ACT.Square,
                                         accum_out=ss[:, i:i + 1]).then_inc(s_sq, 1)

                square(0)
                for i in range(NT + 1):
                    if i + 1 < NT:
                        square(i + 1)
                    if i:
                        act.wait_ge(s_f, 2 * i)
                        nc.scalar.activation(xh[:, :, (i - 1) * P:i * P], xf[:, (i - 1) % 2],
                                             ACT.Copy).then_inc(s_hi, 1)
                for n in range(2):
                    act.wait_ge(m_raw[n], 16)
                    nc.scalar.activation(wh[:, n], raw[:, n], ACT.Copy).then_inc(m_whi, 1)

            @block.gpsimd
            def _(pool):
                nc.gpsimd.memset(mhalf, -0.5).then_inc(s_id, 1)
                nc.gpsimd.memset(ones[:], 1.0).then_inc(s_id, 1)
                nc.gpsimd.memset(ident[:], 0.0).then_inc(s_id, 1)
                pool.wait_ge(s_id, 3)
                nc.gpsimd.affine_select(out=ident[:], in_=ident[:], compare_op=ALU.not_equal, fill=1.0, base=0,
                                        pattern=[[-1, P]], channel_multiplier=1).then_inc(s_const, 1)
                def row_factor(i):
                    pool.wait_ge(s_ms, i + 1)
                    nc.gpsimd.tensor_tensor(rstd[:, i:i + 1], ms[:, i:i + 1], mhalf[:, 0:1],
                                            ALU.pow).then_inc(s_rstd, 1)

                row_factor(0)
                for i in range(NT + 1):
                    if i + 1 < NT:
                        row_factor(i + 1)
                    if i:
                        pool.wait_ge(s_hi, i)
                        cols = slice((i - 1) * P, i * P)
                        nc.gpsimd.tensor_tensor(xl[:, :, cols], xf[:, (i - 1) % 2], xh[:, :, cols].bitcast(F32),
                                                ALU.subtract).then_inc(s_lo, 1)
                for n in range(2):
                    pool.wait_ge(m_whi, n + 1)
                    nc.gpsimd.tensor_tensor(wl[:, n], raw[:, n], wh[:, n].bitcast(F32),
                                            ALU.subtract).then_inc(m_wlo, 1)

            @block.vector
            def _(dve):
                def weigh(i):
                    dve.wait_ge(s_tr, i + 1)
                    if i >= 2:
                        dve.wait_ge(s_lo, i - 1)
                    for j in range(2):
                        w = prm[:, PT_N1 + 4 * j:PT_N1 + 4 * j + 4].unsqueeze(2).to_broadcast([P, 4, P])
                        nc.vector.tensor_tensor(xf[:, i % 2, 4 * j:4 * j + 4, :],
                                                t2[i % 2][j].rearrange("p (k c) -> p k c", k=4), w,
                                                ALU.mult).then_inc(s_f, 1)

                def mean_square(i):
                    dve.wait_ge(s_sq, i + 1)
                    nc.vector.tensor_scalar(ms[:, i:i + 1], ss[:, i:i + 1], 1.0 / D, EPS, ALU.mult,
                                            ALU.add).then_inc(s_ms, 1)

                mean_square(0)
                for i in range(NT):
                    if i + 1 < NT:
                        mean_square(i + 1)
                    if i == 1:
                        dve.wait_ge(s_prt, 1)
                        nc.vector.tensor_copy(prm[:], every[7][:, 0:PT_COLS]).then_inc(s_prm, 1)
                        dve.wait_ge(s_prm, 1)
                    dve.wait_ge(s_rstd, i + 1)
                    nc.vector.tensor_scalar(xn[:, i % 2, :], xs[:, i, :], rstd[:, i:i + 1], None,
                                            ALU.mult).then_inc(s_xn, 1)
                    if i:
                        weigh(i - 1)
                weigh(NT - 1)

            @block.tensor
            def _(pe):
                pe.wait_ge(s_const, 1)
                pe.wait_ge(s_par, 16 * 10)
                for n, (col, m, j) in enumerate(table):
                    last = nc.tensor.transpose(every[7][:, col:col + m], stage[0:m, j, :], ident[0:m, 0:m])
                last.then_inc(s_prt, 1)
                for i in range(NT):
                    pe.wait_ge(s_xn, i + 1)
                    if i >= 2:
                        pe.wait_ge(s_f, 2 * (i - 1))
                    for k in range(KT):
                        last = nc.tensor.transpose(t2[i % 2][k // 4][:, (k % 4) * P:(k % 4 + 1) * P],
                                                   xn[:, i % 2, k * P:(k + 1) * P], ident[:])
                    last.then_inc(s_tr, 1)


def product3(nc, out, wh, wl, xh, xl, halves, first, last):
    n = 0
    parts = [(wh, xh), (wh, xl), (wl, xh)]
    for j, (w, xx) in enumerate(parts):
        for lo, hi in halves:
            mm = nc.tensor.matmul(out[:, lo:hi], w, xx[:, lo:hi], start=first and j == 0, stop=last and j == 2)
    return mm


HALVES = ((0, HALF), (HALF, S))


def mixer(nc, sem, sb, acc, bank_a, bank_b, att_ps, ident, ones, prm, xh, xl,
          w_in2, dn_a_log, dn_dt_bias, dn_onorm_w, conv_d, og_d, oa_d, ob_d, gate_d,
          w_pa2, w_pb2, ring, m_ring, g_ring):
    jobs = mixer_jobs()
    items = mixer_schedule(jobs)
    NJ = len(jobs)
    conv_no = count([n for n, j in enumerate(jobs) if j[0] in ("conv", "z")])
    job_no = {(kind, t): n for n, (kind, t, _) in enumerate(jobs)}

    use_a = {"kv", "kT", "kkD", "kq", "uw", "sq", "so", "ob"} | {f"P{lv}" for lv in range(LEVELS)}
    use_a |= {f"T{lv}" for lv in range(1, LEVELS - 1)}
    use_b = {"kv", "kkD", "U0", "uw", "sq", "so"} | {f"T{lv}" for lv in range(1, LEVELS)}
    dn = [it[1:] for it in items if it[0] == "dn"]
    dn_done = count(dn)
    a_taken = count([d for d in dn if d[0] in use_a])
    b_taken = count([d for d in dn if d[0] in use_b])
    att_no = count([it for it in items if it[0] in ("gates", "gatesum", "vT", "a_qk", "a_pT", "a_pv", "cmbT")])
    order = {it: n for n, it in enumerate(items)}
    unit_no = count(att_units())
    stores = [u for u in att_units() for _ in range(2 if u[0] == 2 else 1)]
    o_stored = {u: 16 * (n + 1) for n, u in enumerate(stores)}
    for g in range(NG - 1):
        nxt = order[("evac", job_no[("q", 2 * g + 4)] if g + 2 < NG else job_no[("gate", 0)])]
        assert order[("a_qk", (g, NT - 1))] < nxt
        assert g + 2 >= NG or order[("a_pv", (g, NT - 1))] < order[("vT", 2 * g + 4)]

    s_const, s_masks, s_small = sem("m_const_step"), sem("m_masks_ready"), sem("m_small_loaded")
    raw, wh, wl = ring
    s_raw, s_whi, s_wlo = m_ring
    g_raw, g_whi, g_wlo = g_ring
    s_acc, s_taken = sem("m_acc_done"), sem("m_acc_taken")
    s_tap0, s_tap, s_silu = sem("m_tap0"), sem("m_tap"), sem("m_silu_done")
    s_cst = [sem("m_conv_stored0"), sem("m_conv_stored1")]
    s_sqr, s_ssq, s_ssum, s_rr = sem("m_squares"), sem("m_ssq_summed"), sem("m_ssq_read"), sem("m_norms")
    s_atpe, s_attk = sem("m_att_filled"), sem("m_att_taken")
    s_bact, s_link, s_gready = sem("m_gate_act"), sem("m_dve_link"), sem("m_gates_ready")
    s_dn, s_a, s_b = sem("m_dn_filled"), sem("m_bank_a_taken"), sem("m_bank_b_taken")
    s_ckkv, s_ckq, s_ckz = sem("m_chunk_kv"), sem("m_chunk_q"), sem("m_chunk_z")
    s_gu, s_kk, s_dtm, s_lm = sem("m_gu"), sem("m_kbe_kd"), sem("m_decay_masked"), sem("m_level_masked")
    s_t0, s_sd, s_osq = sem("m_t0"), sem("m_state_decayed"), sem("m_o_squares")
    s_ov, s_on = sem("m_o_variance"), sem("m_o_normed")
    s_obst = sem("m_ob_stored")
    s_nm, s_p, s_o, s_ost = sem("m_neg_max"), sem("m_probs"), sem("m_o_ready"), sem("m_o_stored")
    s_cl = [sem("m_cmb_loaded0"), sem("m_cmb_loaded1")]
    s_cd, s_ce, s_co, s_cs = sem("m_cmb_diff"), sem("m_cmb_exp"), sem("m_cmb_out"), sem("m_cmb_stored")
    s_gst = [sem("m_gate_stored0"), sem("m_gate_stored1")]

    with ExitStack() as ctx:
        U = sb(ctx, "U", [P, P])
        Ls = sb(ctx, "Ls", [P, P])
        lmask = sb(ctx, "lmask", [P, LEVELS, P])
        amask = sb(ctx, "amask", [P, 2 * P])
        dmask = sb(ctx, "dmask", [P, P])
        onw = sb(ctx, "onw", [P, 1])
        alog = sb(ctx, "alog", [P, NH])
        dtb = sb(ctx, "dtb", [P, NH])
        g_all = sb(ctx, "g_all", [P, NT, NH])
        beta = sb(ctx, "beta", [P, NT, NH])
        dec = sb(ctx, "dec", [P, 3, NT, NH])
        bE = sb(ctx, "bE", [P, NT, NH])
        rr = sb(ctx, "rr", [P, 2, NH, NT])
        rqs = sb(ctx, "rqs", [P, NH, NT])
        rq2 = sb(ctx, "rq2", [P, NH, NT])
        tiny = sb(ctx, "tiny", [P, 4, NH])
        hp64 = sb(ctx, "hp64", [P, 2 * NH * NT])
        eg, ekd, egl = dec[:, 0], dec[:, 1], dec[:, 2]
        ck = sb(ctx, "ck", [P, 4 * NH, P])
        kh, vb, kbe, kd, X1, Pb, DTm, WT, KQd, Lm0, Lm1, Ub, St, o1, sqo, on, obt = (
            sb(ctx, "d_" + name, [P, NH, P]) for name in
            ("kh", "vb", "kbe", "kd", "khT_T_u", "gU_P_vn", "DTm_Sd", "WT_wT", "KQd", "Lm0", "Lm1", "U", "S",
             "o", "sqo", "on", "obt"))
        Lm = (Lm0, Lm1)
        V = [sb(ctx, f"V{j}", [P, NT, AH, DH + 1]) for j in range(2)]
        vt = sb(ctx, "vt", [P, S])
        sc = sb(ctx, "sc", [P, AH, 2 * P])
        mx = sb(ctx, "mx", [P, 2, AH])
        O = sb(ctx, "O", [P, AH, OC])
        PT = sb(ctx, "PT", [P, AH * 2, P])
        cbs = sb(ctx, "cbs", [P, 4, NG, AH])
        cbm = sb(ctx, "cbm", [P, 3, AH])
        with ExitStack() as early:
            cs = sb(early, "cs", [P, 2, S])
            so = sb(early, "so", [P, 2, S])
            sqb = sb(early, "sqb", [P, S])
            bas = sb(early, "bas", [P, S])
            bat = sb(early, "bat", [P, 6, NT, 2 * NH])
        qk = [sb(ctx, f"qk{j}", [P, 4, S]) for j in range(2)]
        cb = [qk[1][:, j, 0:NG * AH * OC].rearrange("p (g h c) -> p g h c", g=NG, h=AH) for j in range(2)]
        gate = [qk[1][:, 2 + j, :] for j in range(2)]
        ocb = PT[:, 0:2, :].rearrange("p a c -> p (a c)")
        oat = PT[:, 4:6, :]

        def bc(ap):
            return ap.unsqueeze(2).to_broadcast([P, NH, P])

        def bh(ap):
            return ap.unsqueeze(1).to_broadcast([P, NH, P])

        A4 = bank_a[:, :].rearrange("p (h c) -> p h c", h=NH)
        B4 = bank_b[:, :].rearrange("p (h c) -> p h c", h=NH)
        att0 = att_ps[:, 0:HALF]
        att4 = att_ps[:, :].rearrange("p (h c) -> p h c", h=AH)

        def dilated(ap, g):
            return ap.rearrange("p (l r) -> p r l", r=GROUPS[g][1])

        def residues(ap, g):
            return ap.rearrange("p (r l) -> p r l", r=GROUPS[g][1])

        def key_tiles(g, i):
            if (g == 0 and i) or (g == 1 and i % 2):
                return [i - 1, i]
            return [i]

        def slot(h):
            return 2 * (h % 2) + h // 2

        with nc.Block() as block:

            @block.sync
            def _(sp):
                sp.dma_start(onw[:], dn_onorm_w[0].rearrange("(p o) -> p o", o=1)).then_inc(s_small, 16)
                sp.dma_start(alog[:], dn_a_log.to_broadcast([P, NH])).then_inc(s_small, 16)
                sp.dma_start(dtb[:], dn_dt_bias.to_broadcast([P, NH])).then_inc(s_small, 16)

                def load_w(n):
                    sp.wait_ge(s_wlo, n - 1)
                    if n < NJ:
                        load_columns(sp, raw[:, n % 2], w_in2[:, jobs[n][2]:jobs[n][2] + P], s_raw[n % 2])
                    else:
                        load_branch_columns(sp, raw[:, n % 2], n - NJ, w_pa2, w_pb2, g_raw[n % 2])

                def load_chunk(first, tiles, c, loaded):
                    sp.dma_start(ck[:, first:first + tiles, :],
                                 conv_d[first:first + tiles, :, c * P:(c + 1) * P].rearrange("t p c -> p t c")
                                 ).then_inc(loaded, 16)

                def load_outputs(i):
                    sp.dma_start(cb[i % 2].rearrange("p g h c -> p g (h c)"),
                                 og_d[:, i * P:(i + 1) * P, :].rearrange("g t c -> t g c")).then_inc(s_cl[i % 2], 16)

                for it in items:
                    kind = it[0]
                    if kind == "w" and 1 <= it[1] <= NJ:
                        load_w(it[1] + 1)
                    if kind == "silu":
                        n, t = it[1], jobs[it[1]][1]
                        sp.wait_ge(s_silu, conv_no[n])
                        sp.dma_start(conv_d[t], so[:, conv_no[n] % 2, :]).then_inc(s_cst[conv_no[n] % 2], 16)
                    if kind == "evac" and jobs[it[1]][0] == "z":
                        n, t = it[1], jobs[it[1]][1]
                        sp.wait_ge(s_taken, n + 1)
                        sp.dma_start(conv_d[3 * NH + t], so[:, conv_no[n] % 2, :]).then_inc(s_cst[conv_no[n] % 2], 16)
                        if t == NH - 1:
                            for j in range(2):
                                sp.wait_ge(s_cst[j], 16 * 2 * NH)
                            load_chunk(3 * NH, NH, 0, s_ckz)
                    if kind == "dn":
                        name, c = it[1:]
                        if name == "kv" and c == 0:
                            for j in range(2):
                                sp.wait_ge(s_cst[j], 16 * 3 * NH // 2)
                            load_chunk(NH, 2 * NH, 0, s_ckkv)
                            load_chunk(0, NH, 0, s_ckq)
                        if name == "kT" and c + 1 < NT:
                            sp.wait_ge(s_dn, dn_done[("kv", c)])
                            load_chunk(NH, 2 * NH, c + 1, s_ckkv)
                        if name == "so" and c + 1 < NT:
                            sp.wait_ge(s_dn, dn_done[("sq", c)])
                            load_chunk(0, NH, c + 1, s_ckq)
                        if name == "ob":
                            sp.wait_ge(s_a, a_taken[(name, c)])
                            sp.dma_start(ob_d[:, :, c * P:(c + 1) * P].rearrange("h p c -> p h c"),
                                         obt[:]).then_inc(s_obst, 16)
                            if c + 1 < NT:
                                load_chunk(3 * NH, NH, c + 1, s_ckz)
                    if kind == "a_pv":
                        g, i = it[1]
                        sp.wait_ge(s_o, unit_no[(g, i)])
                        rows = og_d[g].rearrange("(l r) c -> r l c", r=GROUPS[g][1])
                        src = O[:].rearrange("p h c -> p (h c)")
                        if g == 0:
                            sp.dma_start(rows[0, i * P:(i + 1) * P, :], src).then_inc(s_ost, 16)
                        elif g == 1:
                            sp.dma_start(rows[i // 2, (i % 2) * P:(i % 2 + 1) * P, :], src).then_inc(s_ost, 16)
                        else:
                            for j in range(2):
                                sp.dma_start(rows[2 * i + j], src[j * 64:(j + 1) * 64, :]).then_inc(s_ost, 16)
                            if i == NT - 1:
                                sp.wait_ge(s_ost, o_stored[(g, i)])
                                load_outputs(0)
                                load_outputs(1)
                    if kind == "evac" and jobs[it[1]][0] == "gate":
                        m = jobs[it[1]][1]
                        sp.wait_ge(s_taken, it[1] + 1)
                        sp.dma_start(gate_d[m], gate[m % 2]).then_inc(s_gst[m % 2], 16)
                    if kind == "cmb":
                        i = it[1]
                        if 0 < i < NT - 1:
                            sp.wait_ge(s_co, i)
                            load_outputs(i + 1)
                    if kind == "cmbT":
                        i = it[1]
                        sp.wait_ge(s_attk, att_no[it])
                        sp.dma_start(oa_d[:, :, i * P:(i + 1) * P].rearrange("a p c -> p a c"), oat).then_inc(s_cs, 16)
                sp.wait_ge(s_cs, 16 * NT)
                for j in range(2):
                    sp.wait_ge(s_gst[j], 16 * KT)
                sp.wait_ge(s_obst, 16 * NT)

            @block.gpsimd
            def _(pool):
                g = nc.gpsimd
                steps = 0

                def step(ins):
                    nonlocal steps
                    steps += 1
                    ins.then_inc(s_const, 1)
                    pool.wait_ge(s_const, steps)

                step(g.memset(U[:], 1.0))
                step(g.memset(Ls[:], 1.0))
                step(g.memset(hp64[:], -0.5))
                step(g.affine_select(out=U[:], in_=U[:], compare_op=ALU.is_ge, fill=0.0, base=0, pattern=[[1, P]],
                                     channel_multiplier=-1))
                step(g.affine_select(out=Ls[:], in_=Ls[:], compare_op=ALU.is_gt, fill=0.0, base=0, pattern=[[-1, P]],
                                     channel_multiplier=1))
                step(g.memset(lmask[:], 0.0))
                for lv in range(LEVELS):
                    size = 1 << lv
                    nb = P // (2 * size)
                    v = lmask[:, lv, :].rearrange("p (b t s) -> p b t s", t=2, s=size)[:, :, 1, :]
                    step(g.memset(v, 1.0))
                    step(g.affine_select(out=v, in_=v, compare_op=ALU.is_ge, fill=0.0, base=0,
                                         pattern=[[-2 * size, nb], [0, size]], channel_multiplier=1))
                    step(g.affine_select(out=v, in_=v, compare_op=ALU.is_gt, fill=0.0, base=size,
                                         pattern=[[2 * size, nb], [0, size]], channel_multiplier=-1))
                step(g.memset(amask[:], 0.0))
                step(g.affine_select(out=amask[:], in_=amask[:], compare_op=ALU.is_ge, fill=NEG, base=0,
                                     pattern=[[1, 2 * P]], channel_multiplier=-1))
                step(g.affine_select(out=amask[:], in_=amask[:], compare_op=ALU.is_ge, fill=NEG, base=P,
                                     pattern=[[-1, 2 * P]], channel_multiplier=1))
                step(g.memset(dmask[:], 0.0))
                step(g.affine_select(out=dmask[:], in_=dmask[:], compare_op=ALU.is_ge, fill=NEG, base=0,
                                     pattern=[[-1, P]], channel_multiplier=1))
                step(g.affine_select(out=dmask[:, 0:64], in_=dmask[:, 0:64], compare_op=ALU.is_ge, fill=NEG, base=63,
                                     pattern=[[0, 64]], channel_multiplier=-1))
                step(g.memset(St[:], 0.0))
                for j in range(2):
                    step(g.memset(V[j][:, :, :, DH:DH + 1], 1.0))
                g.memset(tiny[:], 0.0).then_inc(s_masks, 1)

                def level_mask(lv, c):
                    g.tensor_tensor(Lm[lv % 2][:], WT[:], bh(lmask[:, lv, :]), ALU.mult).then_inc(s_lm, 1)

                def out_norm(c):
                    pool.wait_ge(s_ov, 2 * c + 2)
                    g.tensor_tensor(tiny[:, 2, :], tiny[:, 1, :], hp64[:, 0:NH], ALU.pow).then_inc(s_on, 1)
                    pool.wait_ge(s_on, 3 * c + 1)
                    g.tensor_tensor(tiny[:, 3, :], tiny[:, 2, :], rqs[:, :, c], ALU.mult).then_inc(s_on, 1)
                    pool.wait_ge(s_on, 3 * c + 2)
                    if c:
                        pool.wait_ge(s_dn, dn_done[("ob", c - 1)])
                    g.tensor_tensor(on[:], o1[:], bc(tiny[:, 3, :]), ALU.mult).then_inc(s_on, 1)

                for it in items:
                    kind = it[0]
                    if kind == "w":
                        n = it[1]
                        if 2 <= n < NJ:
                            pool.wait_ge(s_whi, n + 1)
                            g.tensor_tensor(wl[:, n % 2], raw[:, n % 2], wh[:, n % 2].bitcast(F32),
                                            ALU.subtract).then_inc(s_wlo, 1)
                        if n >= NJ:
                            pool.wait_ge(g_whi, n - NJ + 1)
                            g.tensor_tensor(wl[:, n % 2, 0:NBR], raw[:, n % 2, 0:NBR],
                                            wh[:, n % 2, 0:NBR].bitcast(F32), ALU.subtract).then_inc(g_wlo, 1)
                    if kind == "silu" and jobs[it[1]][1] < 2 * NH:
                        n, t = it[1], jobs[it[1]][1]
                        pool.wait_ge(s_silu, conv_no[n])
                        if t:
                            pool.wait_ge(s_ssq, t)
                        g.tensor_tensor(sqb[:], so[:, conv_no[n] % 2, :], so[:, conv_no[n] % 2, :],
                                        ALU.mult).then_inc(s_sqr, 1)
                    if kind == "rnorm":
                        pool.wait_ge(s_ssum, 1)
                        flat = rr[:].rearrange("p a h c -> p (a h c)")
                        g.tensor_tensor(flat, flat, hp64[:], ALU.pow).then_inc(s_rr, 1)
                        pool.wait_ge(s_rr, 1)
                        g.tensor_scalar(rqs[:], rr[:, 0], DK ** -0.5, 0.0, ALU.mult, ALU.add).then_inc(s_rr, 1)
                        pool.wait_ge(s_rr, 2)
                        g.tensor_tensor(rq2[:], rqs[:], rqs[:], ALU.mult).then_inc(s_rr, 1)
                        pool.wait_ge(s_rr, 3)
                        g.tensor_scalar(rq2[:], rq2[:], 1.0 / DK, 0.0, ALU.mult, ALU.add).then_inc(s_rr, 1)
                    if kind == "dn":
                        name, c = it[1:]
                        if name == "kv":
                            if c == 0:
                                pool.wait_ge(s_gready, 1)
                            else:
                                pool.wait_ge(s_dn, dn_done[("so", c - 1)])
                            g.tensor_tensor(Pb[:], bh(U[:]), bc(g_all[:, c, :]), ALU.mult).then_inc(s_gu, 1)
                            pool.wait_ge(s_a, a_taken[("kv", c)])
                            g.tensor_tensor(kbe[:], kh[:], bc(bE[:, c, :]), ALU.mult)
                            g.tensor_tensor(kd[:], kh[:], bc(ekd[:, c, :]), ALU.mult).then_inc(s_kk, 1)
                        if name == "kkD":
                            pool.wait_ge(s_b, b_taken[(name, c)])
                            g.tensor_tensor(DTm[:], DTm[:], bh(U[:]), ALU.mult).then_inc(s_dtm, 1)
                            pool.wait_ge(s_a, a_taken[(name, c)])
                            level_mask(0, c)
                            level_mask(1, c)
                        if name[0] == "P" and int(name[1:]) + 2 < LEVELS:
                            pool.wait_ge(s_dn, dn_done[(name, c)])
                            level_mask(int(name[1:]) + 2, c)
                        if name == "uw":
                            pool.wait_ge(s_a, a_taken[("kq", c)])
                            g.tensor_tensor(DTm[:], St[:], bc(egl[:, c, :]), ALU.mult).then_inc(s_sd, 1)
                        if name == "so":
                            pool.wait_ge(s_b, b_taken[(name, c)])
                            g.tensor_tensor(sqo[:], o1[:], o1[:], ALU.mult).then_inc(s_osq, 1)
                        if name == "kT" and c:
                            out_norm(c - 1)
                        if name == "ob" and c == NT - 1:
                            out_norm(c)

            @block.scalar
            def _(act):
                g = nc.scalar
                for it in items:
                    kind = it[0]
                    if kind == "w":
                        n = it[1]
                        if n >= 2:
                            act.wait_ge(s_acc, n - 1)
                        if 2 <= n < NJ:
                            act.wait_ge(s_raw[n % 2], 16 * (n // 2 + 1))
                            g.activation(wh[:, n % 2], raw[:, n % 2], ACT.Copy).then_inc(s_whi, 1)
                        if n >= NJ:
                            act.wait_ge(g_raw[n % 2], 32)
                            g.activation(wh[:, n % 2, 0:NBR], raw[:, n % 2, 0:NBR], ACT.Copy).then_inc(g_whi, 1)
                    if kind == "evac":
                        n = it[1]
                        jk, t, _ = jobs[n]
                        a = acc[n % 2]
                        act.wait_ge(s_acc, n + 1)
                        if n:
                            act.wait_ge(s_taken, n)
                        if jk == "ba":
                            g.activation(bas[0:2 * NH, :], a[0:2 * NH, :], ACT.Copy).then_inc(s_taken, 1)
                        if jk == "conv":
                            w = PT_DN + (CONV - 1) * 3 * NH + t
                            g.activation(cs[:, conv_no[n] % 2, :], a[:], ACT.Copy,
                                         scale=prm[:, w:w + 1]).then_inc(s_tap0, 1)
                        if jk == "z":
                            m = conv_no[n]
                            act.wait_ge(s_cst[m % 2], 16 * ((m - 1) // 2))
                            g.activation(so[:, m % 2, :], a[:], ACT.Silu).then_inc(s_taken, 1)
                        if jk in ("q", "k"):
                            grp = t // 2
                            if jk == "q" and t == 0:
                                for j in range(2):
                                    act.wait_ge(s_cst[j], 16 * 2 * NH)
                                act.wait_ge(s_ssq, 2 * NH)
                                act.wait_ge(s_gready, 1)
                            if jk == "q" and grp == 2:
                                act.wait_ge(s_atpe, att_no[("a_qk", (0, NT - 1))])
                            g.activation(residues(qk[grp % 2][:, (0 if jk == "q" else 2) + t % 2, :], grp),
                                         dilated(a[:], grp), ACT.Copy).then_inc(s_taken, 1)
                        if jk == "v":
                            if t:
                                act.wait_ge(s_atpe, att_no[("vT", t - 1)])
                            g.activation(residues(vt[:], t // 2), dilated(a[:], t // 2), ACT.Copy).then_inc(s_taken, 1)
                        if jk == "gate":
                            if t == 0:
                                act.wait_ge(s_atpe, att_no[("a_qk", (1, NT - 1))])
                            if t >= 2:
                                act.wait_ge(s_gst[t % 2], 16 * (t // 2))
                            g.activation(gate[t % 2], a[:], ACT.Sigmoid).then_inc(s_taken, 1)
                    if kind == "silu":
                        n, m = it[1], conv_no[it[1]]
                        act.wait_ge(s_taken, n + 1)
                        if m > 2:
                            act.wait_ge(s_cst[m % 2], 16 * ((m - 1) // 2))
                            act.wait_ge(s_sqr, min(m - 2, 2 * NH))
                        g.activation(so[:, m % 2, :], cs[:, m % 2, :], ACT.Silu).then_inc(s_silu, 1)
                    if kind == "gates":
                        act.wait_ge(s_small, 48)
                        act.wait_ge(s_link, 2)
                        g.activation(beta[:], bat[:, 0, :, 0:NH], ACT.Sigmoid).then_inc(s_bact, 1)
                        g.activation(bat[:, 3, :, 0:NH], bat[:, 1, :, 0:NH], ACT.Abs).then_inc(s_bact, 1)
                        act.wait_ge(s_bact, 2)
                        g.activation(bat[:, 4, :, 0:NH], bat[:, 3, :, 0:NH], ACT.Exp, scale=-1.0).then_inc(s_bact, 1)
                        g.activation(bat[:, 3, 0, NH:2 * NH], alog[:], ACT.Exp).then_inc(s_bact, 1)
                        act.wait_ge(s_link, 4)
                        g.activation(bat[:, 5, :, 0:NH], bat[:, 4, :, 0:NH], ACT.Ln).then_inc(s_bact, 1)
                    if kind == "gatesum":
                        act.wait_ge(s_atpe, att_no[it])
                        g.activation(dec[:].rearrange("p a c h -> p (a c h)"), att0[:, 0:3 * NT * NH],
                                     ACT.Exp).then_inc(s_attk, 1)
                    if kind == "dn":
                        name, c = it[1:]
                        if name == "kT":
                            act.wait_ge(s_dn, dn_done[(name, c)])
                            g.activation(X1[:], A4, ACT.Copy).then_inc(s_a, 1)
                        if name == "kkD":
                            act.wait_ge(s_dn, dn_done[(name, c)])
                            g.activation(DTm[:], B4, ACT.Exp).then_inc(s_b, 1)
                        if name == "uw":
                            act.wait_ge(s_dn, dn_done[(name, c)])
                            g.activation(X1[:], A4, ACT.Copy).then_inc(s_a, 1)
                    if kind == "a_qk":
                        grp, i = it[1]
                        nk = P * len(key_tiles(grp, i))
                        act.wait_ge(s_nm, unit_no[it[1]])
                        for q in range(AH):
                            last = g.activation(sc[:, q, 0:nk], sc[:, q, 0:nk], ACT.Exp, bias=mx[:, 1, q:q + 1],
                                                scale=ATT_SCALE)
                        last.then_inc(s_p, 1)
                    if kind == "a_pT":
                        nb = AH * len(key_tiles(*it[1]))
                        act.wait_ge(s_atpe, att_no[it])
                        g.activation(PT[:, 0:nb, :].rearrange("p b c -> p (b c)"), att_ps[:, 0:nb * P],
                                     ACT.Copy).then_inc(s_attk, 1)
                    if kind == "cmb":
                        i = it[1]
                        act.wait_ge(s_cd, i + 1)
                        g.activation(cbs[:, 1], cbs[:, 0], ACT.Exp, scale=ATT_SCALE).then_inc(s_ce, 1)
                    if kind == "cmbT":
                        i = it[1]
                        act.wait_ge(s_atpe, att_no[it])
                        if i:
                            act.wait_ge(s_cs, 16 * i)
                        g.activation(oat.rearrange("p a c -> p (a c)"), att0[:, 0:2 * P], ACT.Copy).then_inc(s_attk, 1)

            @block.vector
            def _(dve):
                g = nc.vector
                links = 0

                def link(ins):
                    nonlocal links
                    links += 1
                    ins.then_inc(s_link, 1)
                    dve.wait_ge(s_link, links)

                def variance(c):
                    dve.wait_ge(s_osq, c + 1)
                    link(g.reduce_sum(tiny[:, 0, :], sqo[:], AX))
                    g.tensor_tensor(tiny[:, 1, :], tiny[:, 0, :], rq2[:, :, c], ALU.mult).then_inc(s_ov, 1)
                    dve.wait_ge(s_ov, 2 * c + 1)
                    g.tensor_scalar(tiny[:, 1, :], tiny[:, 1, :], EPS, None, ALU.add).then_inc(s_ov, 1)

                for it in items:
                    kind = it[0]
                    if kind == "gatesum":
                        dve.wait_ge(s_masks, 1)
                    if kind == "evac" and jobs[it[1]][0] == "conv":
                        n, t = it[1], jobs[it[1]][1]
                        m = conv_no[n]
                        a, c0 = acc[n % 2], cs[:, m % 2, :]
                        dve.wait_ge(s_tap0, m)
                        for j in range(1, CONV):
                            w = PT_DN + (CONV - 1 - j) * 3 * NH + t
                            ins = g.scalar_tensor_tensor(c0[:, j:S], a[:, 0:S - j], prm[:, w:w + 1], c0[:, j:S],
                                                         ALU.mult, ALU.add)
                            if j < CONV - 1:
                                ins.then_inc(s_tap, 1)
                                dve.wait_ge(s_tap, (CONV - 2) * (m - 1) + j)
                            else:
                                ins.then_inc(s_taken, 1)
                    if kind == "rnorm":
                        dve.wait_ge(s_ssq, 2 * NH)
                        g.tensor_scalar(rr[:].rearrange("p a h c -> p (a h c)"), bank_b[:, 0:2 * NH * NT], EPS, None,
                                        ALU.add).then_inc(s_ssum, 1)
                    if kind == "gates":
                        dve.wait_ge(s_small, 48)
                        dve.wait_ge(s_atpe, att_no[it])
                        ins = g.tensor_copy(bat[:, 0].rearrange("p c h -> p (c h)"), att0[:, 0:NT * 2 * NH])
                        link(ins)
                        link(g.tensor_tensor(bat[:, 1, :, 0:NH], bat[:, 0, :, NH:2 * NH],
                                             dtb[:].unsqueeze(1).to_broadcast([P, NT, NH]), ALU.add))
                        link(g.tensor_scalar(bat[:, 2, :, 0:NH], bat[:, 1, :, 0:NH], 0.0, None, ALU.max))
                        dve.wait_ge(s_bact, 4)
                        link(g.tensor_scalar(bat[:, 4, :, 0:NH], bat[:, 4, :, 0:NH], 1.0, None, ALU.add))
                        dve.wait_ge(s_bact, 5)
                        link(g.tensor_tensor(bat[:, 2, :, 0:NH], bat[:, 2, :, 0:NH], bat[:, 5, :, 0:NH], ALU.add))
                        link(g.tensor_scalar(bat[:, 2, :, 0:NH], bat[:, 2, :, 0:NH], -1.0, None, ALU.mult))
                        g.tensor_tensor(g_all[:], bat[:, 2, :, 0:NH],
                                        bat[:, 3, 0, NH:2 * NH].unsqueeze(1).to_broadcast([P, NT, NH]),
                                        ALU.mult).then_inc(s_attk, 1)
                    if kind == "gatesum":
                        dve.wait_ge(s_attk, att_no[it])
                        g.tensor_tensor(bE[:], beta[:], eg, ALU.mult).then_inc(s_gready, 1)
                    if kind == "dn":
                        name, c = it[1:]
                        if name == "kT" and c:
                            variance(c - 1)
                        if name == "ob" and c == NT - 1:
                            variance(c)
                        dve.wait_ge(s_dn, dn_done[(name, c)])
                        if name == "kv":
                            if c == 0:
                                dve.wait_ge(s_rr, 4)
                            g.tensor_tensor(vb[:], B4, bc(beta[:, c, :]), ALU.mult).then_inc(s_b, 1)
                            g.tensor_tensor(kh[:], A4, bc(rr[:, 1, :, c]), ALU.mult).then_inc(s_a, 1)
                        if name == "kkD":
                            dve.wait_ge(s_dtm, c + 1)
                            g.tensor_tensor(WT[:], A4, DTm[:], ALU.mult).then_inc(s_a, 1)
                        if name == "kq":
                            g.tensor_tensor(KQd[:], A4, DTm[:], ALU.mult).then_inc(s_a, 1)
                        if name[0] == "P":
                            g.tensor_tensor(Pb[:], A4, bc(beta[:, c, :]), ALU.mult).then_inc(s_a, 1)
                        if name == "P0":
                            dve.wait_ge(s_a, a_taken[(name, c)])
                            g.tensor_tensor(X1[:], bh(ident[:]), Pb[:], ALU.subtract).then_inc(s_t0, 1)
                        if name == "U0":
                            g.tensor_tensor(Ub[:], bh(ident[:]), B4, ALU.subtract).then_inc(s_b, 1)
                        if name[0] == "T":
                            g.tensor_tensor(Ub[:], Ub[:], B4, ALU.subtract).then_inc(s_b, 1)
                            if (name, c) in a_taken:
                                g.tensor_tensor(X1[:], X1[:], A4, ALU.subtract).then_inc(s_a, 1)
                        if name == "uw":
                            g.tensor_copy(WT[:], B4).then_inc(s_b, 1)
                        if name == "sq":
                            g.tensor_tensor(Pb[:], X1[:], A4, ALU.subtract).then_inc(s_a, 1)
                            if c:
                                dve.wait_ge(s_on, 3 * c)
                            g.tensor_tensor(o1[:], B4, bc(eg[:, c, :]), ALU.mult).then_inc(s_b, 1)
                        if name == "so":
                            dve.wait_ge(s_sd, c + 1)
                            g.tensor_tensor(St[:], DTm[:], A4, ALU.add).then_inc(s_a, 1)
                            dve.wait_ge(s_b, b_taken[("sq", c)])
                            g.tensor_tensor(o1[:], o1[:], B4, ALU.add).then_inc(s_b, 1)
                        if name == "ob":
                            dve.wait_ge(s_ckz, 16 * (c + 1))
                            if c:
                                dve.wait_ge(s_obst, 16 * c)
                            g.scalar_tensor_tensor(obt[:], A4, onw[:, 0:1], ck[:, 3 * NH:4 * NH, :], ALU.mult,
                                                   ALU.mult).then_inc(s_a, 1)
                    if kind == "vT":
                        t = it[1]
                        dve.wait_ge(s_atpe, att_no[it])
                        g.tensor_copy(V[t // 2 % 2][:, :, 2 * (t % 2):2 * (t % 2) + 2, 0:DH],
                                      att_ps[:].rearrange("p (i h c) -> p i h c", i=NT, h=2)).then_inc(s_attk, 1)
                    if kind == "a_qk":
                        grp, i = it[1]
                        u = unit_no[it[1]]
                        nk = P * len(key_tiles(grp, i))
                        mask = dmask[:] if grp == 2 else amask[:, 2 * P - nk:2 * P]
                        dve.wait_ge(s_atpe, att_no[it])
                        g.tensor_tensor(sc[:, :, 0:nk], att4[:, :, 0:nk],
                                        mask.unsqueeze(1).to_broadcast([P, AH, nk]), ALU.add).then_inc(s_attk, 1)
                        dve.wait_ge(s_attk, att_no[it])
                        link(g.reduce_max(mx[:, 0, :], sc[:, :, 0:nk], AX))
                        g.tensor_scalar(mx[:, 1, :], mx[:, 0, :], -ATT_SCALE, None, ALU.mult).then_inc(s_nm, 1)
                    if kind == "a_pv":
                        u = unit_no[it[1]]
                        dve.wait_ge(s_atpe, att_no[it])
                        if u > 1:
                            dve.wait_ge(s_ost, o_stored[att_units()[u - 2]])
                        g.tensor_copy(O[:, :, 0:DH + 1],
                                      att0[:, 0:AH * (DH + 1)].rearrange("p (h c) -> p h c", h=AH)).then_inc(s_attk, 1)
                        g.tensor_copy(O[:, :, DH + 1].rearrange("p (i a) -> p a i", a=2),
                                      mx[:, 0, :].rearrange("p (a i) -> p a i", a=2)).then_inc(s_o, 1)
                    if kind == "cmb":
                        i = it[1]
                        X = cb[i % 2]
                        dve.wait_ge(s_cl[i % 2], 16 * (i // 2 + 1))
                        top = X[:, :, :, DH + 1]
                        link(g.tensor_tensor(cbm[:, 0], top[:, 0], top[:, 1], ALU.max))
                        link(g.tensor_tensor(cbm[:, 1], cbm[:, 0], top[:, 2], ALU.max))
                        g.tensor_tensor(cbs[:, 0], top, cbm[:, 1].unsqueeze(1).to_broadcast([P, NG, AH]),
                                        ALU.subtract).then_inc(s_cd, 1)
                        dve.wait_ge(s_ce, i + 1)
                        link(g.tensor_tensor(cbs[:, 2], cbs[:, 1], X[:, :, :, DH], ALU.mult))
                        link(g.tensor_tensor(cbm[:, 0], cbs[:, 2, 0], cbs[:, 2, 1], ALU.add))
                        link(g.tensor_tensor(cbm[:, 1], cbm[:, 0], cbs[:, 2, 2], ALU.add))
                        link(g.reciprocal(cbm[:, 2], cbm[:, 1]))
                        link(g.tensor_tensor(cbs[:, 3], cbs[:, 1], cbm[:, 2].unsqueeze(1).to_broadcast([P, NG, AH]),
                                             ALU.mult))
                        for q in range(NG):
                            ins = g.tensor_tensor(X[:, q, :, 0:DH], X[:, q, :, 0:DH],
                                                  cbs[:, 3, q].unsqueeze(2).to_broadcast([P, AH, DH]), ALU.mult)
                        link(ins)
                        oc = ocb.rearrange("p (h c) -> p h c", h=AH)
                        if i:
                            dve.wait_ge(s_atpe, att_no[("cmbT", i - 1)])
                        link(g.tensor_tensor(oc, X[:, 0, :, 0:DH], X[:, 1, :, 0:DH], ALU.add))
                        g.tensor_tensor(oc, oc, X[:, 2, :, 0:DH], ALU.add).then_inc(s_co, 1)

            @block.tensor
            def _(pe):
                t_ = nc.tensor
                def each_head(out4, lhs, rhs, transpose=False):
                    for h in range(NH):
                        r = ident[:] if rhs is None else rhs[:, h, :]
                        if transpose:
                            last = t_.transpose(out4[:, h, :], lhs[:, h, :], ident[:])
                        else:
                            last = t_.matmul(out4[:, h, :], lhs[:, h, :], r, start=True, stop=True)
                    return last

                for it in items:
                    kind = it[0]
                    if kind == "mm":
                        n, k = it[1], it[2]
                        if k == 0:
                            pe.wait_ge(s_wlo, n + 1)
                            if n >= 2:
                                pe.wait_ge(s_taken, n - 1)
                        mm = product3(nc, acc[n % 2], wh[:, n % 2, k, :], wl[:, n % 2, k, :], xh[:, k, :], xl[:, k, :],
                                      HALVES, k == 0, k == KT - 1)
                        if k == KT - 1:
                            mm.then_inc(s_acc, 1)
                    if kind == "ssq":
                        t = it[1]
                        pe.wait_ge(s_sqr, t + 1)
                        for c in range(NT):
                            last = t_.matmul(bank_b[:, t * NT + c:t * NT + c + 1], sqb[:, c * P:(c + 1) * P],
                                             ones[:, 0:1], start=True, stop=True)
                        last.then_inc(s_ssq, 1)
                    if it in att_no:
                        if att_no[it] > 1:
                            pe.wait_ge(s_attk, att_no[it] - 1)
                    if kind == "gates":
                        pe.wait_ge(s_taken, 1)
                        for c in range(NT):
                            last = t_.transpose(att0[:, c * 2 * NH:(c + 1) * 2 * NH], bas[0:2 * NH, c * P:(c + 1) * P],
                                                ident[0:2 * NH, 0:2 * NH])
                        last.then_inc(s_atpe, 1)
                    if kind == "gatesum":
                        pe.wait_ge(s_masks, 1)
                        for j, m in enumerate((U, Ls, ones)):
                            last = t_.matmul(att0[:, j * NT * NH:(j + 1) * NT * NH], m[:],
                                             g_all[:].rearrange("p c h -> p (c h)"), start=True, stop=True)
                        last.then_inc(s_atpe, 1)
                    if kind == "vT":
                        pe.wait_ge(s_taken, job_no[("v", it[1])] + 1)
                        for i in range(NT):
                            last = t_.transpose(att_ps[:, i * P:(i + 1) * P], vt[:, i * P:(i + 1) * P], ident[:])
                        last.then_inc(s_atpe, 1)
                    if kind == "a_qk":
                        grp, i = it[1]
                        tiles = key_tiles(grp, i)
                        keys = slice(tiles[0] * P, (tiles[-1] + 1) * P)
                        for h in (0, 2, 1, 3):
                            rows = slice((h % 2) * DH, (h % 2 + 1) * DH)
                            last = t_.matmul(att4[:, slot(h), 0:P * len(tiles)],
                                             qk[grp % 2][rows, h // 2, i * P:(i + 1) * P],
                                             qk[grp % 2][rows, 2 + h // 2, keys], start=True, stop=True)
                        last.then_inc(s_atpe, 1)
                    if kind == "a_pT":
                        grp, i = it[1]
                        nb = len(key_tiles(grp, i))
                        pe.wait_ge(s_p, unit_no[it[1]])
                        for q in range(AH):
                            for b in range(nb):
                                j = q * nb + b
                                last = t_.transpose(att_ps[:, j * P:(j + 1) * P], sc[:, q, b * P:(b + 1) * P], ident[:])
                        last.then_inc(s_atpe, 1)
                    if kind == "a_pv":
                        grp, i = it[1]
                        tiles = key_tiles(grp, i)
                        for h in range(AH):
                            for b, tile in enumerate(tiles):
                                last = t_.matmul(att0[:, h * (DH + 1):(h + 1) * (DH + 1)],
                                                 PT[:, slot(h) * len(tiles) + b, :], V[grp % 2][:, tile, h, :],
                                                 start=b == 0, stop=b == len(tiles) - 1)
                        last.then_inc(s_atpe, 1)
                    if kind == "cmbT":
                        pe.wait_ge(s_co, it[1] + 1)
                        for j in range(2):
                            last = t_.transpose(att0[:, j * P:(j + 1) * P], ocb[:, j * P:(j + 1) * P], ident[:])
                        last.then_inc(s_atpe, 1)
                    if kind == "dn":
                        name, c = it[1:]
                        key = (name, c)
                        if key in a_taken and a_taken[key] > 1:
                            pe.wait_ge(s_a, a_taken[key] - 1)
                        if key in b_taken and b_taken[key] > 1:
                            pe.wait_ge(s_b, b_taken[key] - 1)
                        if name == "kv":
                            if c == 0:
                                pe.wait_ge(s_ssum, 1)
                            pe.wait_ge(s_ckkv, 16 * (c + 1))
                            each_head(A4, ck[:, NH:2 * NH, :], None, True)
                            last = each_head(B4, ck[:, 2 * NH:3 * NH, :], None, True)
                        if name == "kT":
                            last = each_head(A4, kh, None, True)
                        if name == "kkD":
                            pe.wait_ge(s_gu, c + 1)
                            each_head(A4, X1, X1)
                            last = t_.matmul(bank_b[:, :], Ls[:], Pb[:].rearrange("p h c -> p (h c)"), start=True,
                                             stop=True)
                        if name == "kq":
                            pe.wait_ge(s_ckq, 16 * (c + 1))
                            last = each_head(A4, X1, ck[:, 0:NH, :])
                        if name[0] == "P":
                            lv = int(name[1:])
                            pe.wait_ge(s_lm, c * LEVELS + lv + 1)
                            if lv == 1:
                                pe.wait_ge(s_t0, c + 1)
                            last = each_head(A4, Lm[lv % 2], X1 if lv else None)
                        if name == "U0":
                            pe.wait_ge(s_a, a_taken[("P0", c)])
                            last = each_head(B4, Pb, None)
                        if name[0] == "T":
                            pe.wait_ge(s_a, a_taken[("P" + name[1:], c)])
                            if key in a_taken:
                                each_head(A4, Ub, Pb)
                            last = each_head(B4, Pb, Ub)
                        if name == "uw":
                            pe.wait_ge(s_b, b_taken[(f"T{LEVELS - 1}", c)])
                            pe.wait_ge(s_kk, c + 1)
                            each_head(A4, Ub, vb)
                            last = each_head(B4, kbe, Ub)
                        if name == "sq":
                            each_head(A4, WT, St)
                            last = each_head(B4, ck[:, 0:NH, :], St)
                        if name == "so":
                            each_head(A4, kd, Pb)
                            last = each_head(B4, KQd, Pb)
                        if name == "ob":
                            pe.wait_ge(s_on, 3 * (c + 1))
                            last = each_head(A4, on, None, True)
                        last.then_inc(s_dn, 1)


def merge_and_project(nc, sem, sb, acc, every, ident, small, prm, xh, xl, w_pa2, w_pb2, w_o2, oa_d, ob_d,
                      gate_d, xd, h_d, w_up2, ring, g_ring, u_ring):
    ss, ms, rstd, mhalf = small[:, 0:8], small[:, 8:16], small[:, 16:24], small[:, 24:32]
    NA, NB = AO // P, DW // P
    NW = NBR
    PAIR = 2
    s_o = [sem(f"g_o_loaded{k}") for k in range(NBR)]
    s_oh, s_ol = sem("g_o_high"), sem("g_o_low")
    s_gate = [sem("g_gates_loaded0"), sem("g_gates_loaded1")]
    raw, wh, wl = ring
    s_raw, s_whi, s_wlo = g_ring
    u_raw, u_whi, u_wlo = u_ring
    NJ = len(mixer_jobs())
    s_pa, s_pb = sem("g_pa_done"), sem("g_pb_done")
    s_y1, s_t, s_y2, s_yh, s_yl = (sem("g_first_term"), sem("g_second_term"), sem("g_y_ready"), sem("g_y_high"),
                                   sem("g_y_low"))
    s_praw = [sem(f"p_w_loaded{j}") for j in range(KT // PAIR)]
    s_phi, s_plo, s_x = sem("p_w_high"), sem("p_w_low"), sem("p_x_loaded")
    s_k, s_bank, s_mm, s_h = sem("p_k_done"), sem("p_bank_done"), sem("p_product"), sem("p_h_added")
    s_sq, s_ms, s_rstd, s_xn = sem("p_squares"), sem("p_mean_square"), sem("p_rstd"), sem("p_scaled")
    s_tr, s_f, s_hi, s_lo, s_st = (sem("p_transposed"), sem("p_weighted"), sem("p_high"), sem("p_low"),
                                   sem("p_h_stored"))
    with ExitStack() as ctx:
        oh = sb(ctx, "g_oh", [P, NW, S], F32R)
        ol = sb(ctx, "g_ol", [P, NW, S], F32R)
        gates = sb(ctx, "g_gates", [P, 2, 2, S])
        yt = sb(ctx, "g_y", [P, S])
        praw = sb(ctx, "p_raw", [P, KT, HALF])
        h = sb(ctx, "p_h", [P, NT, D])
        o_in = h
        ph = [oh[:, k // 2, (k % 2) * HALF:(k % 2 + 1) * HALF] for k in range(KT)]
        pl = [ol[:, k // 2, (k % 2) * HALF:(k % 2 + 1) * HALF] for k in range(KT)]
        xn, junk = [gates[:, 0, 0, :], gates[:, 1, 1, :]], gates[:, 0, 1, :]
        xf = gates[:, 1, 0, :].rearrange("p (k c) -> p k c", k=KT)
        t2 = [[every[0], every[1]], [every[2], every[3]]]

        def slot(m):
            return (NJ + m) % 2

        with nc.Block() as block:

            @block.sync
            def _(sp):
                def load(m):
                    if m >= 2:
                        sp.wait_ge(s_wlo, m - 1)
                        load_branch_columns(sp, raw[:, slot(m)], m, w_pa2, w_pb2, s_raw[slot(m)])
                        sp.wait_ge(s_y2, m - 1)
                    sp.dma_start(gates[:, m % 2], gate_d.rearrange("(j m) p c -> m p j c", j=2)[m]
                                 ).then_inc(s_gate[m % 2], 16)

                def load_w(half, j):
                    if half:
                        sp.wait_ge(s_plo, (j + 1) * PAIR)
                    rows = slice(j * PAIR * P, (j + 1) * PAIR * P)
                    sp.dma_start(praw[:, j * PAIR:(j + 1) * PAIR, :],
                                 w_o2[rows, half * HALF:(half + 1) * HALF].rearrange("(k p) c -> p k c", p=P)
                                 ).then_inc(s_praw[j], 16)

                for k in range(NW):
                    sp.dma_start(o_in[:, k, :], oa_d[k] if k < NA else ob_d[k - NA]).then_inc(s_o[k], 16)
                    if k == 0:
                        load(0)
                load(1)
                for j in range(KT // PAIR):
                    load_w(0, j)
                for m in range(2, KT):
                    load(m)
                sp.wait_ge(s_ol, NW)
                for st in range(NT):
                    sp.dma_start(h[:, st, :], xd[st * P:(st + 1) * P, :]).then_inc(s_x, 16)
                for j in range(2):
                    sp.wait_ge(s_wlo, KT)
                    load_columns(sp, raw[:, j], w_up2[:, j * FF:j * FF + P], u_raw[j])
                for j in range(KT // PAIR):
                    load_w(1, j)
                for st in range(NT):
                    sp.wait_ge(s_h, NT + st + 1)
                    sp.dma_start(h_d[st * P:(st + 1) * P, :], h[:, st, :]).then_inc(s_st, 16)
                sp.wait_ge(s_st, 16 * NT)

            @block.scalar
            def _(act):
                def split(m):
                    act.wait_ge(s_raw[slot(m)], 32 * (m // 2 + 1))
                    act.wait_ge(s_pb, m - 1)
                    nc.scalar.activation(wh[:, slot(m), 0:NW], raw[:, slot(m), 0:NW], ACT.Copy).then_inc(s_whi, 1)

                def split_w(half, k):
                    act.wait_ge(s_praw[k // PAIR], 16 * (half + 1))
                    nc.scalar.activation(ph[k], praw[:, k, :], ACT.Copy).then_inc(s_phi, 1)

                for k in range(NW):
                    act.wait_ge(s_o[k], 16)
                    nc.scalar.activation(oh[:, k, :], o_in[:, k, :], ACT.Copy).then_inc(s_oh, 1)
                for m in range(KT):
                    if 0 < m < KT - 1:
                        split(m + 1)
                    if m == KT - 1:
                        act.wait_ge(s_pa, KT)
                        for k in range(2 * NA):
                            split_w(0, k)
                    act.wait_ge(s_y2, m + 1)
                    nc.scalar.activation(xh[:, m, :], yt[:], ACT.Copy).then_inc(s_yh, 1)
                act.wait_ge(s_pb, KT)
                for k in range(2 * NA, KT):
                    split_w(0, k)
                for k in range(KT):
                    if k < KT - 1:
                        act.wait_ge(s_k, k + 1)
                    else:
                        act.wait_ge(s_bank, NT)
                    split_w(1, k)
                for j in range(2):
                    act.wait_ge(u_raw[j], 16)
                    nc.scalar.activation(wh[:, j], raw[:, j], ACT.Copy).then_inc(u_whi, 1)
                for st in range(NT + 1):
                    if st < NT:
                        act.wait_ge(s_h, NT + st + 1)
                        if st:
                            act.wait_ge(s_sq, st)
                        nc.scalar.activation(junk, h[:, st, :], ACT.Square,
                                             accum_out=ss[:, st:st + 1]).then_inc(s_sq, 1)
                    if st:
                        act.wait_ge(s_f, 2 * st)
                        nc.scalar.activation(xh[:, :, (st - 1) * P:st * P], xf, ACT.Copy).then_inc(s_hi, 1)

            @block.gpsimd
            def _(pool):
                for m in range(2, KT):
                    pool.wait_ge(s_whi, m + 1)
                    nc.gpsimd.tensor_tensor(wl[:, slot(m), 0:NW], raw[:, slot(m), 0:NW],
                                            wh[:, slot(m), 0:NW].bitcast(F32), ALU.subtract).then_inc(s_wlo, 1)
                for n in range(2 * KT):
                    pool.wait_ge(s_phi, n + 1)
                    nc.gpsimd.tensor_tensor(pl[n % KT], praw[:, n % KT, :], ph[n % KT].bitcast(F32),
                                            ALU.subtract).then_inc(s_plo, 1)
                for j in range(2):
                    pool.wait_ge(u_whi, j + 1)
                    nc.gpsimd.tensor_tensor(wl[:, j], raw[:, j], wh[:, j].bitcast(F32),
                                            ALU.subtract).then_inc(u_wlo, 1)
                for st in range(NT + 1):
                    if st < NT:
                        pool.wait_ge(s_ms, st + 1)
                        nc.gpsimd.tensor_tensor(rstd[:, st:st + 1], ms[:, st:st + 1], mhalf[:, 0:1],
                                                ALU.pow).then_inc(s_rstd, 1)
                    if st:
                        pool.wait_ge(s_hi, st)
                        cols = slice((st - 1) * P, st * P)
                        nc.gpsimd.tensor_tensor(xl[:, :, cols], xf, xh[:, :, cols].bitcast(F32),
                                                ALU.subtract).then_inc(s_lo, 1)

            @block.vector
            def _(dve):
                for k in range(NW):
                    dve.wait_ge(s_oh, k + 1)
                    nc.vector.tensor_tensor(ol[:, k, :], o_in[:, k, :], oh[:, k, :].bitcast(F32),
                                            ALU.subtract).then_inc(s_ol, 1)
                for m in range(KT):
                    y, g = yt[:], gates[:, m % 2]
                    dve.wait_ge(s_pa, m + 1)
                    dve.wait_ge(s_gate[m % 2], 16 * (m // 2 + 1))
                    if m:
                        dve.wait_ge(s_yl, m)
                    nc.vector.tensor_tensor(y, g[:, 0, :], acc[0][:], ALU.mult).then_inc(s_y1, 1)
                    dve.wait_ge(s_pb, m + 1)
                    nc.vector.tensor_tensor(g[:, 1, :], g[:, 1, :], acc[1][:], ALU.mult).then_inc(s_t, 1)
                    dve.wait_ge(s_t, m + 1)
                    nc.vector.tensor_tensor(y, y, g[:, 1, :], ALU.add).then_inc(s_y2, 1)
                    dve.wait_ge(s_yh, m + 1)
                    nc.vector.tensor_tensor(xl[:, m, :], y, xh[:, m, :].bitcast(F32), ALU.subtract).then_inc(s_yl, 1)
                dve.wait_ge(s_x, 16 * NT)

                def add(half, st):
                    cols = slice(half * HALF, (half + 1) * HALF)
                    nc.vector.tensor_tensor(h[:, st, cols], h[:, st, cols], every[st], ALU.add).then_inc(s_h, 1)

                def weigh(st):
                    dve.wait_ge(s_tr, st + 1)
                    if st:
                        dve.wait_ge(s_lo, st)
                    for j in range(2):
                        w = prm[:, PT_N2 + 4 * j:PT_N2 + 4 * j + 4].unsqueeze(2).to_broadcast([P, 4, P])
                        nc.vector.tensor_tensor(xf[:, 4 * j:4 * j + 4, :],
                                                t2[st % 2][j].rearrange("p (k c) -> p k c", k=4), w,
                                                ALU.mult).then_inc(s_f, 1)

                for st in range(NT):
                    dve.wait_ge(s_bank, st + 1)
                    add(0, st)
                for st in range(NT):
                    dve.wait_ge(s_mm, st + 1)
                    add(1, st)
                    if st >= 2:
                        weigh(st - 2)
                    dve.wait_ge(s_sq, st + 1)
                    nc.vector.tensor_scalar(ms[:, st:st + 1], ss[:, st:st + 1], 1.0 / D, EPS, ALU.mult,
                                            ALU.add).then_inc(s_ms, 1)
                    dve.wait_ge(s_rstd, st + 1)
                    if st >= 2:
                        dve.wait_ge(s_tr, st - 1)
                    nc.vector.tensor_scalar(xn[st % 2], h[:, st, :], rstd[:, st:st + 1], None, ALU.mult).then_inc(s_xn, 1)
                weigh(NT - 2)
                weigh(NT - 1)

            @block.tensor
            def _(pe):
                def rows_of(out, m, w0, n):
                    for k in range(n):
                        if m == 0:
                            pe.wait_ge(s_ol, w0 + k + 1)
                        mm = product3(nc, out, wh[:, slot(m), w0 + k, :], wl[:, slot(m), w0 + k, :], oh[:, w0 + k, :],
                                      ol[:, w0 + k, :], HALVES, k == 0, k == n - 1)
                    return mm

                def product(st, k, first, last):
                    rows = slice(st * P, (st + 1) * P)
                    for j, (a, b) in enumerate(((xh, ph), (xh, pl), (xl, ph))):
                        mm = nc.tensor.matmul(every[st], a[:, k, rows], b[k], start=first and j == 0,
                                              stop=last and j == 2)
                    return mm

                def transposes(st):
                    pe.wait_ge(s_xn, st + 1)
                    if st >= 2:
                        pe.wait_ge(s_f, 2 * (st - 1))
                    else:
                        pe.wait_ge(s_h, NT + 2 * (st + 1))
                    for k in range(KT):
                        last = nc.tensor.transpose(t2[st % 2][k // 4][:, (k % 4) * P:(k % 4 + 1) * P],
                                                   xn[st % 2][:, k * P:(k + 1) * P], ident[:])
                    last.then_inc(s_tr, 1)

                for m in range(KT):
                    pe.wait_ge(s_wlo, m + 1)
                    if m:
                        pe.wait_ge(s_y1, m)
                    rows_of(acc[0], m, 0, NA).then_inc(s_pa, 1)
                    if m:
                        pe.wait_ge(s_t, m)
                    rows_of(acc[1], m, NA, NB).then_inc(s_pb, 1)
                for k in range(KT):
                    pe.wait_ge(s_plo, k + 1)
                    pe.wait_ge(s_yl, k + 1)
                    for st in range(NT):
                        if k == 0 and st % 2 == 0 and st < 4:
                            pe.wait_ge(s_t if st else s_y1, KT)
                        mm = product(st, k, k == 0, k == KT - 1)
                        if k == KT - 1:
                            mm.then_inc(s_bank, 1)
                    if k < KT - 1:
                        mm.then_inc(s_k, 1)
                for st in range(NT):
                    pe.wait_ge(s_h, st + 1)
                    for k in range(KT):
                        if st == 0:
                            pe.wait_ge(s_plo, KT + k + 1)
                        mm = product(st, k, k == 0, k == KT - 1)
                    mm.then_inc(s_mm, 1)
                    if st == 2:
                        transposes(0)
                    if st == 4:
                        transposes(1)
                    if st >= 4:
                        transposes(st - 2)
                transposes(NT - 2)
                transposes(NT - 1)


def ffn(nc, sem, sb, acc, every, prm, small, xh, xl, w_up2, w_dn2, h_d, final_norm_w, outd, ring, u_ring, f_ring):
    with ExitStack() as ctx:
        glu = sb(ctx, "glu", [P, FT, S])
        ffn_up(nc, sem, sb, acc, prm, xh, xl, glu, w_up2, w_dn2, ring, u_ring, f_ring)
        ffn_down(nc, sem, sb, every, small, xh, xl, glu, w_dn2, h_d, final_norm_w, outd, ring, f_ring)


def down_slots(ring):
    return [[t[:, j, 0:HALF // P, :].rearrange("p a c -> p (a c)") for j in range(2)] for t in ring]


def ffn_up(nc, sem, sb, acc, prm, xh, xl, glu, w_up2, w_dn2, ring, u_ring, f_ring):
    raw, wh, wl = ring
    s_raw, s_whi, s_wlo = u_ring
    f_raw, f_whi, f_wlo = f_ring
    down = down_slots(ring)
    s_acc, s_tap0, s_tap, s_taken = sem("u_acc_done"), sem("u_tap0"), sem("u_tap1"), sem("u_acc_taken")
    s_silu, s_glu = sem("u_silu"), sem("u_glu")
    with ExitStack() as ctx:
        cv = sb(ctx, "u_conv", [P, 2, S])
        sg = sb(ctx, "u_silu", [P, S])
        with nc.Block() as block:

            @block.sync
            def _(sp):
                def turn(i):
                    for j in range(2):
                        sp.wait_ge(s_wlo, 2 * i - 1 + j)
                        load_columns(sp, raw[:, j], w_up2[:, bass.ds(i * P + j * FF, P)], s_raw[j])

                with sp.Fori(1, FT) as i:
                    turn(i)
                for j in range(2):
                    sp.wait_ge(s_wlo, 2 * FT - 1 + j)
                    sp.dma_start(down[0][j], w_dn2[j * P:(j + 1) * P, 0:HALF]).then_inc(f_raw[j], 16)

            @block.scalar
            def _(act):
                def split(i, j):
                    act.wait_ge(s_raw[j], 16 * i + 16)
                    act.wait_ge(s_acc, 2 * i - 1 + j)
                    nc.scalar.activation(wh[:, j], raw[:, j], ACT.Copy).then_inc(s_whi, 1)

                def split_down(j):
                    act.wait_ge(f_raw[j], 16)
                    act.wait_ge(s_acc, 2 * FT - 1 + j)
                    nc.scalar.activation(down[1][j], down[0][j], ACT.Copy).then_inc(f_whi, 1)

                def turn(i, first=False, last=False):
                    if not first:
                        split(i, 1)
                    for j in range(2):
                        act.wait_ge(s_acc, 2 * i + 1 + j)
                        if not first:
                            act.wait_ge(s_glu if j else s_silu, i)
                        w = PT_FFN + (FCONV - 1) * 2 * FT + j * FT
                        b = PT_BIAS + j * FT
                        nc.scalar.activation(cv[:, j, :], acc[j][:], ACT.Identity, bias=prm[:, bass.ds(b + i, 1)],
                                             scale=prm[:, bass.ds(w + i, 1)]).then_inc(s_tap0, 1)
                        if j == 0:
                            if not last:
                                split(i + 1, 0)
                            act.wait_ge(s_taken, 2 * i + 1)
                            if not first:
                                act.wait_ge(s_glu, i)
                            nc.scalar.activation(sg[:], cv[:, 0, :], ACT.Silu).then_inc(s_silu, 1)
                            if last:
                                split_down(0)

                turn(0, True)
                with act.Fori(1, FT - 1) as i:
                    turn(i)
                turn(FT - 1, last=True)
                split_down(1)

            @block.gpsimd
            def _(pool):
                def turn(i):
                    for j in range(2):
                        pool.wait_ge(s_whi, 2 * i + 1 + j)
                        nc.gpsimd.tensor_tensor(wl[:, j], raw[:, j], wh[:, j].bitcast(F32),
                                                ALU.subtract).then_inc(s_wlo, 1)

                with pool.Fori(1, FT) as i:
                    turn(i)

            @block.vector
            def _(dve):
                def turn(i):
                    for j in range(2):
                        dve.wait_ge(s_tap0, 2 * i + 1 + j)
                        for tap in (1, 2):
                            w = PT_FFN + (FCONV - 1 - tap) * 2 * FT + j * FT
                            ins = nc.vector.scalar_tensor_tensor(cv[:, j, tap:S], acc[j][:, 0:S - tap],
                                                                 prm[:, bass.ds(w + i, 1)], cv[:, j, tap:S],
                                                                 ALU.mult, ALU.add)
                            if tap == 1:
                                ins.then_inc(s_tap, 1)
                                dve.wait_ge(s_tap, 2 * i + 1 + j)
                            else:
                                ins.then_inc(s_taken, 1)
                    dve.wait_ge(s_taken, 2 * i + 2)
                    dve.wait_ge(s_silu, i + 1)
                    nc.vector.tensor_tensor(glu[:, bass.ds(i, 1), :], sg[:].unsqueeze(1), cv[:, 1:2, :],
                                            ALU.mult).then_inc(s_glu, 1)

                with dve.Fori(0, FT) as i:
                    turn(i)
                for j in range(2):
                    dve.wait_ge(f_whi, j + 1)
                    nc.vector.tensor_tensor(down[2][j], down[0][j], down[1][j].bitcast(F32),
                                            ALU.subtract).then_inc(f_wlo, 1)

            @block.tensor
            def _(pe):
                def turn(i, first=False):
                    for j in range(2):
                        pe.wait_ge(s_wlo, 2 * i + 1 + j)
                        if not first:
                            pe.wait_ge(s_taken, 2 * i - 1 + j)
                        for k in range(KT):
                            mm = product3(nc, acc[j], wh[:, j, k, :], wl[:, j, k, :], xh[:, k, :], xl[:, k, :],
                                          HALVES, k == 0, k == KT - 1)
                        mm.then_inc(s_acc, 1)

                turn(0, True)
                with pe.Fori(1, FT) as i:
                    turn(i)


def ffn_down(nc, sem, sb, every, small, xh, xl, glu, w_dn2, h_d, final_norm_w, outd, ring, f_ring):
    ss, ms, rstd, mhalf = small[:, 0:8], small[:, 8:16], small[:, 16:24], small[:, 24:32]
    NHALF = D // HALF
    s_raw, s_whi, s_wlo = f_ring
    raw, wh, wl = down_slots(ring)
    s_gh, s_gl = sem("f_glu_high"), sem("f_glu_low")
    s_k, s_bank, s_sum = sem("f_k_done"), sem("f_bank_done"), sem("f_summed")
    s_h, s_fw = sem("f_h_loaded"), sem("f_norm_loaded")
    s_sq, s_ms, s_rstd, s_y, s_out = (sem("f_squares"), sem("f_mean_square"), sem("f_rstd"), sem("f_scaled"),
                                      sem("f_out_stored"))
    with ExitStack() as ctx:
        rows_of_h = sb(ctx, "f_h", [P, NT - 1, NHALF, HALF])
        h = [rows_of_h[:, st] for st in range(NT - 1)]
        h.append(ring[0][:, :, KT // 2:KT, :].rearrange("p a b c -> p a (b c)"))
        gh, gl = xh[:, 0:2, :], xl[:, 0:2, :]
        FW_TILE = 2
        fw = glu[:, FW_TILE, :].rearrange("p (a c) -> p a c", a=NHALF)
        junk = glu[:, 0, :].rearrange("p (a c) -> p a c", a=NHALF)
        with nc.Block() as block:
            NQ = FT // 2

            @block.sync
            def _(sp):
                def load(half, q):
                    for j in range(2):
                        sp.wait_ge(s_wlo, half * FT + 2 * q - 1 + j)
                        sp.dma_start(raw[j], w_dn2[bass.ds((2 * q + j) * P, P), half * HALF:(half + 1) * HALF]
                                     ).then_inc(s_raw[j], 16)

                for st in range(NT):
                    sp.dma_start(h[st], h_d[st * P:(st + 1) * P, :].rearrange("p (a c) -> p a c", a=NHALF)).then_inc(s_h, 16)
                with sp.Fori(1, NQ) as q:
                    load(0, q)
                with sp.Fori(0, NQ) as q:
                    load(1, q)
                sp.wait_ge(s_gl, FT + FW_TILE + 1)
                sp.dma_start(fw, final_norm_w.rearrange("(a c) -> a c", a=NHALF).unsqueeze(0)
                             .to_broadcast([P, NHALF, HALF])).then_inc(s_fw, 16)
                for st in range(NT):
                    sp.wait_ge(s_y, st + 1)
                    sp.dma_start(outd[st * P:(st + 1) * P, :].rearrange("p (a c) -> p a c", a=NHALF), h[st]).then_inc(s_out, 16)
                sp.wait_ge(s_out, 16 * NT)

            @block.scalar
            def _(act):
                def turn(half, q, first=False):
                    for j in range(2):
                        kk = half * FT + 2 * q + j
                        if not first:
                            act.wait_ge(s_k, kk - 1 - half)
                        elif half and j == 0:
                            act.wait_ge(s_k, FT - 1)
                        elif half:
                            act.wait_ge(s_bank, NT)
                        nc.scalar.activation(gh[:, j, :].unsqueeze(1), glu[:, bass.ds(2 * q + j, 1), :],
                                             ACT.Copy).then_inc(s_gh, 1)
                        act.wait_ge(s_raw[j], (half * NQ + q) * 16 + 16)
                        nc.scalar.activation(wh[j], raw[j], ACT.Copy).then_inc(s_whi, 1)

                for j in range(2):
                    nc.scalar.activation(gh[:, j, :].unsqueeze(1), glu[:, j:j + 1, :], ACT.Copy).then_inc(s_gh, 1)
                with act.Fori(1, NQ) as q:
                    turn(0, q)
                turn(1, 0, True)
                with act.Fori(1, NQ) as q:
                    turn(1, q)
                for st in range(NT):
                    act.wait_ge(s_sum, NT + st + 1)
                    if st:
                        act.wait_ge(s_sq, st)
                    nc.scalar.activation(junk, h[st], ACT.Square, accum_out=ss[:, st:st + 1]).then_inc(s_sq, 1)

            @block.gpsimd
            def _(pool):
                def turn(half, q):
                    for j in range(2):
                        pool.wait_ge(s_gh, half * FT + 2 * q + j + 1)
                        nc.gpsimd.tensor_tensor(gl[:, j, :].unsqueeze(1), glu[:, bass.ds(2 * q + j, 1), :],
                                                gh[:, j, :].bitcast(F32).unsqueeze(1), ALU.subtract).then_inc(s_gl, 1)

                for half in range(NHALF):
                    with pool.Fori(0, NQ) as q:
                        turn(half, q)
                for st in range(NT):
                    pool.wait_ge(s_ms, st + 1)
                    nc.gpsimd.tensor_tensor(rstd[:, st:st + 1], ms[:, st:st + 1], mhalf[:, 0:1],
                                            ALU.pow).then_inc(s_rstd, 1)

            @block.vector
            def _(dve):
                def low(half, q, j):
                    dve.wait_ge(s_whi, half * FT + 2 * q + j + 1)
                    nc.vector.tensor_tensor(wl[j], raw[j], wh[j].bitcast(F32), ALU.subtract).then_inc(s_wlo, 1)

                def add(half, st):
                    dve.wait_ge(s_bank, half * NT + st + 1)
                    nc.vector.tensor_tensor(h[st][:, half, :], h[st][:, half, :], every[st], ALU.add
                                            ).then_inc(s_sum, 1)

                def mean_square(st):
                    dve.wait_ge(s_sq, st + 1)
                    nc.vector.tensor_scalar(ms[:, st:st + 1], ss[:, st:st + 1], 1.0 / D, EPS, ALU.mult,
                                            ALU.add).then_inc(s_ms, 1)

                def scale(st):
                    dve.wait_ge(s_rstd, st + 1)
                    nc.vector.scalar_tensor_tensor(h[st], h[st], rstd[:, st:st + 1], fw, ALU.mult,
                                                   ALU.mult).then_inc(s_y, 1)

                with dve.Fori(1, NQ) as q:
                    low(0, q, 0)
                    low(0, q, 1)
                dve.wait_ge(s_h, 16 * NT)
                low(1, 0, 0)
                for st in range(NT):
                    add(0, st)
                low(1, 0, 1)
                with dve.Fori(1, NQ) as q:
                    low(1, q, 0)
                    low(1, q, 1)
                dve.wait_ge(s_fw, 16)
                for st in range(NT + 2):
                    if st < NT:
                        add(1, st)
                    if 1 <= st <= NT:
                        mean_square(st - 1)
                    if st >= 2:
                        scale(st - 2)

            @block.tensor
            def _(pe):
                def turn(half, q, first=False, last=False):
                    for j in range(2):
                        kk = half * FT + 2 * q + j
                        pe.wait_ge(s_gl, kk + 1)
                        pe.wait_ge(s_wlo, kk + 1)
                        for st in range(NT):
                            if first and j == 0 and half:
                                pe.wait_ge(s_sum, st + 1)
                            rows = slice(st * P, (st + 1) * P)
                            for n, (a, b) in enumerate(((gh, wh), (gh, wl), (gl, wh))):
                                mm = nc.tensor.matmul(every[st], a[:, j, rows], b[j], start=first and j == 0 and n == 0,
                                                      stop=last and j == 1 and n == 2)
                            if last and j == 1:
                                mm.then_inc(s_bank, 1)
                        if not (last and j == 1):
                            mm.then_inc(s_k, 1)

                for half in range(NHALF):
                    turn(half, 0, first=True)
                    with pe.Fori(1, NQ - 1) as q:
                        turn(half, q)
                    turn(half, NQ - 1, last=True)


_OUTS = [((1, S, D), "float32")]
_INS = ["x", "norm1_w", "w_in", "dn_conv_w", "dn_a_log", "dn_dt_bias", "dn_onorm_w", "w_pa", "w_pb", "w_o",
        "norm2_w", "w_up", "ffn_conv_w", "ffn_conv_b", "w_down", "final_norm_w"]


def kernel(**inputs):
    import numpy as _np
    import concourse.bacc as _bacc
    from concourse import mybir as _mybir
    from concourse.bass_utils import run_bass_kernel_spmd as _run

    nc = _bacc.Bacc("TRN2", target_bir_lowering=False, num_devices=1)
    arrays, args = {}, []
    for name in _INS:
        a = _np.ascontiguousarray(inputs[name])
        arrays[f"in_{name}_dram"] = a
        args.append(nc.dram_tensor(f"in_{name}_dram", a.shape, _mybir.dt.from_np(a.dtype), kind="ExternalInput").ap())
    for i, (shape, dtype) in enumerate(_OUTS):
        dt = _mybir.dt.from_np(_np.dtype(dtype))
        args.append(nc.dram_tensor(f"out_{i}_dram", shape, dt, kind="ExternalOutput").ap())
    build(nc, *args)
    r = _run(nc, [arrays], core_ids=[0])
    return r.results[0]["out_0_dram"]
```
